# Optimizing a Trainium2 kernel written in Bass

```python
import jax, jax.numpy as jnp
from jax import lax
import numpy as np

D_MODEL = 1024
BATCH = 1
SEQ = 512
DEPTH = 1

D_MIX = D_MODEL
M_HEADS = 4
M_HEAD_DIM = 128
D_MLSTM = M_HEADS * M_HEAD_DIM
D_GMLP = D_MIX - D_MLSTM
G_GROUPS = 4
G_DIM = D_GMLP // G_GROUPS
CHUNK = 128
CONV_K = 4
N_EXPERTS = 32
TOP_K = 4
D_FF = D_MODEL
SWIGLU_LIMIT = 7.0
SWIGLU_ALPHA = 1.702
MOE_BLOCK = 128
EPS = 1e-6
PROJ_SIZES = (D_MLSTM, D_MLSTM, D_MLSTM, D_MLSTM, M_HEADS, M_HEADS, D_GMLP, D_GMLP)
D_PROJ = sum(PROJ_SIZES)

kernel_name = "hybrid_mlstm_gmlp_moe"

def rms_norm(x, gain):
    xf = x.astype(jnp.float32)
    y = xf * lax.rsqrt(jnp.mean(xf * xf, axis=-1, keepdims=True) + EPS)
    return (y * gain).astype(x.dtype)

def layer_norm(x, gain):
    xf = x.astype(jnp.float32)
    mu = jnp.mean(xf, axis=-1, keepdims=True)
    xc = xf - mu
    y = xc * lax.rsqrt(jnp.mean(xc * xc, axis=-1, keepdims=True) + EPS)
    return (y * gain).astype(x.dtype)

def causal_dwconv(x, w):
    S = x.shape[1]
    xp = jnp.pad(x, ((0, 0), (CONV_K - 1, 0), (0, 0)))
    y = xp[:, 0:S] * w[0]
    for j in range(1, CONV_K):
        y = y + xp[:, j:j + S] * w[j]
    return y

def mlstm_chunkwise(q, k, v, i_pre, f_pre):
    B, S, H, DH = q.shape
    nc = S // CHUNK
    out_dtype = q.dtype

    def chunks(t):
        return t.astype(jnp.float32).reshape(B, nc, CHUNK, H, DH).transpose(0, 3, 1, 2, 4)

    q = chunks(q)
    k = chunks(k) * (DH ** -0.5)
    v = chunks(v)
    log_i = i_pre.astype(jnp.float32).reshape(B, nc, CHUNK, H).transpose(0, 3, 1, 2)
    log_f = jax.nn.log_sigmoid(f_pre.astype(jnp.float32)).reshape(B, nc, CHUNK, H).transpose(0, 3, 1, 2)
    b = jnp.cumsum(log_f, axis=-1)
    b_last = b[..., -1]

    g = b_last[..., None] - b + log_i
    m_loc = jnp.max(g, axis=-1)
    w_loc = jnp.exp(g - m_loc[..., None])
    C_loc = jnp.einsum('bhcs,bhcsv,bhcsk->bhcvk', w_loc, v, k)
    n_loc = jnp.einsum('bhcs,bhcsk->bhck', w_loc, k)

    def step(carry, inp):
        C, n, m = carry
        Cl, nl, ml, bl = inp
        m_new = jnp.maximum(bl + m, ml)
        a = jnp.exp(bl + m - m_new)
        c = jnp.exp(ml - m_new)
        C_new = a[..., None, None] * C + c[..., None, None] * Cl
        n_new = a[..., None] * n + c[..., None] * nl
        return (C_new, n_new, m_new), (C, n, m)

    init = (jnp.zeros((B, H, DH, DH), jnp.float32),
            jnp.zeros((B, H, DH), jnp.float32),
            jnp.zeros((B, H), jnp.float32))
    xs = (jnp.moveaxis(C_loc, 2, 0), jnp.moveaxis(n_loc, 2, 0),
          jnp.moveaxis(m_loc, 2, 0), jnp.moveaxis(b_last, 2, 0))
    _, (C_prev, n_prev, m_prev) = lax.scan(step, init, xs)
    C_prev = jnp.moveaxis(C_prev, 0, 2)
    n_prev = jnp.moveaxis(n_prev, 0, 2)
    m_prev = jnp.moveaxis(m_prev, 0, 2)

    causal = jnp.tril(jnp.ones((CHUNK, CHUNK), dtype=bool))
    D = jnp.where(causal, b[..., :, None] - b[..., None, :] + log_i[..., None, :], -jnp.inf)
    a_inter = b + m_prev[..., None]
    m = jnp.maximum(a_inter, jnp.max(D, axis=-1))
    W = jnp.exp(D - m[..., None]) * jnp.einsum('bhctd,bhcsd->bhcts', q, k)
    inter = jnp.exp(a_inter - m)
    num = (jnp.einsum('bhcts,bhcsv->bhctv', W, v)
           + inter[..., None] * jnp.einsum('bhcvk,bhctk->bhctv', C_prev, q))
    den = jnp.sum(W, axis=-1) + inter * jnp.einsum('bhck,bhctk->bhct', n_prev, q)
    h = num / jnp.maximum(jnp.abs(den), jnp.exp(-m))[..., None]
    return h.transpose(0, 2, 3, 1, 4).reshape(B, S, H, DH).astype(out_dtype)

def spatial_gating(u, vg, ln_gain, w_spatial, b_spatial, out_gain):
    B, S, _ = u.shape
    nc = S // CHUNK
    u = jax.nn.gelu(u)
    vg = layer_norm(jax.nn.gelu(vg), ln_gain)
    vc = vg.reshape(B, nc, CHUNK, G_GROUPS, G_DIM)
    causal = jnp.tril(jnp.ones((CHUNK, CHUNK), dtype=bool))
    w = jnp.where(causal[None], w_spatial, 0.0)
    mixed = jnp.einsum('gts,bcsgd->bctgd', w, vc) + b_spatial.T[:, :, None]
    return rms_norm(u * mixed.reshape(B, S, D_GMLP), out_gain)

def hybrid_mixer(xn, w_in, conv_qk, b_igate, b_fgate, mlstm_norm_gain,
                 gmlp_ln_gain, w_spatial, b_spatial, gmlp_out_gain, w_out):
    B, S, _ = xn.shape
    proj = xn @ w_in
    splits = np.cumsum(PROJ_SIZES)[:-1].tolist()
    q, k, v, o, ig, fg, u, vg = jnp.split(proj, splits, axis=-1)
    qk = jax.nn.silu(causal_dwconv(jnp.concatenate([q, k], axis=-1), conv_qk))
    q, k = jnp.split(qk, 2, axis=-1)
    heads = lambda t: t.reshape(B, S, M_HEADS, M_HEAD_DIM)
    h = mlstm_chunkwise(heads(q), heads(k), heads(v), ig + b_igate, fg + b_fgate)
    h = layer_norm(h, mlstm_norm_gain)
    h_m = jax.nn.sigmoid(o) * h.reshape(B, S, D_MLSTM)
    h_g = spatial_gating(u, vg, gmlp_ln_gain, w_spatial, b_spatial, gmlp_out_gain)
    return jnp.concatenate([h_m, h_g], axis=-1) @ w_out

def moe_ffn(x, w_router, b_router, w_up, b_up, w_down, b_down):
    T, D = x.shape
    logits = (x @ w_router + b_router).astype(jnp.float32)
    top_logit, top_idx = lax.top_k(logits, TOP_K)
    gate = jax.nn.softmax(top_logit, axis=-1).astype(x.dtype)
    A = T * TOP_K
    flat_e = top_idx.reshape(A)
    flat_tok = jnp.arange(A, dtype=jnp.int32) // TOP_K
    flat_g = gate.reshape(A)
    order = jnp.argsort(flat_e)
    se, stok, sg = flat_e[order], flat_tok[order], flat_g[order]
    counts = jnp.bincount(flat_e, length=N_EXPERTS)
    padded = (counts + MOE_BLOCK - 1) // MOE_BLOCK * MOE_BLOCK
    start = jnp.cumsum(counts) - counts
    pend = jnp.cumsum(padded)
    pstart = pend - padded
    dest = pstart[se] + (jnp.arange(A) - start[se])
    n_blocks = -(-A // MOE_BLOCK) + N_EXPERTS
    nbuf = n_blocks * MOE_BLOCK
    tok_buf = jnp.zeros((nbuf,), jnp.int32).at[dest].set(stok)
    g_buf = jnp.zeros((nbuf,), x.dtype).at[dest].set(sg)
    block_e = jnp.minimum(jnp.searchsorted(pend, jnp.arange(n_blocks) * MOE_BLOCK, side='right'),
                          N_EXPERTS - 1)

    def block_fn(args):
        toks, g, e = args
        xb = x[toks]
        hb = xb @ w_up[e] + b_up[e]
        h_glu, h_lin = jnp.split(hb, 2, axis=-1)
        h_glu = jnp.minimum(h_glu, SWIGLU_LIMIT)
        h_lin = jnp.clip(h_lin, -SWIGLU_LIMIT, SWIGLU_LIMIT)
        act = h_glu * jax.nn.sigmoid(SWIGLU_ALPHA * h_glu) * (h_lin + 1.0)
        return (act @ w_down[e] + b_down[e]) * g[:, None]

    yb = lax.map(block_fn, (tok_buf.reshape(n_blocks, MOE_BLOCK),
                            g_buf.reshape(n_blocks, MOE_BLOCK), block_e))
    return jax.ops.segment_sum(yb.reshape(nbuf, D), tok_buf, num_segments=T)

def setup_inputs(seed: int = 0) -> dict:
    key = jax.random.key(seed)
    ks = jax.random.split(key, 24)
    nrm = lambda k, shape, s: jax.random.normal(k, shape, jnp.float32) * s
    L = DEPTH
    return {
        "x": nrm(ks[0], (BATCH, SEQ, D_MODEL), 1.0),
        "norm1_gain": 1.0 + nrm(ks[1], (L, D_MODEL), 0.05),
        "w_in": nrm(ks[2], (L, D_MODEL, D_PROJ), D_MODEL ** -0.5),
        "conv_qk": nrm(ks[3], (L, CONV_K, 2 * D_MLSTM), CONV_K ** -0.5),
        "b_igate": nrm(ks[4], (L, M_HEADS), 0.1),
        "b_fgate": jnp.linspace(3.0, 6.0, M_HEADS, dtype=jnp.float32)[None] + nrm(ks[5], (L, M_HEADS), 0.1),
        "mlstm_norm_gain": 1.0 + nrm(ks[6], (L, M_HEADS, M_HEAD_DIM), 0.05),
        "gmlp_ln_gain": 1.0 + nrm(ks[7], (L, D_GMLP), 0.05),
        "w_spatial": nrm(ks[8], (L, G_GROUPS, CHUNK, CHUNK), CHUNK ** -0.5),
        "b_spatial": 1.0 + nrm(ks[9], (L, G_GROUPS, CHUNK), 0.1),
        "gmlp_out_gain": 1.0 + nrm(ks[10], (L, D_GMLP), 0.05),
        "w_out": nrm(ks[11], (L, D_MIX, D_MODEL), D_MIX ** -0.5),
        "norm2_gain": 1.0 + nrm(ks[12], (L, D_MODEL), 0.05),
        "w_router": nrm(ks[13], (L, D_MODEL, N_EXPERTS), D_MODEL ** -0.5),
        "b_router": nrm(ks[14], (L, N_EXPERTS), 0.01),
        "w_up": nrm(ks[15], (L, N_EXPERTS, D_MODEL, 2 * D_FF), D_MODEL ** -0.5),
        "b_up": nrm(ks[16], (L, N_EXPERTS, 2 * D_FF), 0.02),
        "w_down": nrm(ks[17], (L, N_EXPERTS, D_FF, D_MODEL), D_FF ** -0.5),
        "b_down": nrm(ks[18], (L, N_EXPERTS, D_MODEL), 0.02),
        "final_gain": 1.0 + nrm(ks[19], (D_MODEL,), 0.05),
    }

def reference(x, norm1_gain, w_in, conv_qk, b_igate, b_fgate, mlstm_norm_gain, gmlp_ln_gain,
              w_spatial, b_spatial, gmlp_out_gain, w_out, norm2_gain, w_router, b_router,
              w_up, b_up, w_down, b_down, final_gain):
    B, S, D = x.shape
    h = x
    for l in range(DEPTH):
        xn = rms_norm(h, norm1_gain[l])
        h = h + hybrid_mixer(xn, w_in[l], conv_qk[l], b_igate[l], b_fgate[l], mlstm_norm_gain[l],
                             gmlp_ln_gain[l], w_spatial[l], b_spatial[l], gmlp_out_gain[l], w_out[l])
        hn = rms_norm(h, norm2_gain[l])
        h = h + moe_ffn(hn.reshape(B * S, D), w_router[l], b_router[l], w_up[l], b_up[l],
                        w_down[l], b_down[l]).reshape(B, S, D)
    return rms_norm(h, final_gain)


_drawn_inputs = setup_inputs


def setup_inputs(seed=0):
    import zlib

    import numpy as np

    out = dict(_drawn_inputs(seed))
    spreads = {}
    factors = {'b_igate': 64.0, 'b_up': 6.246, 'b_down': 7.218}
    for name, (base, spread) in spreads.items():
        noise = np.random.default_rng([zlib.crc32(name.encode()), seed]).standard_normal(out[name].shape)
        drawn = base * np.exp(spread * noise) if base else spread * noise
        out[name] = __import__('jax').numpy.asarray(drawn.astype(out[name].dtype))
    for name, factor in factors.items():
        out[name] = (out[name] * factor).astype(out[name].dtype)
    return out
```

```python
import concourse.bass as bass
from concourse import mybir
from contextlib import ExitStack

f32 = mybir.dt.float32
i32 = mybir.dt.int32
u32 = mybir.dt.uint32
ALU = mybir.AluOpType
ACT = mybir.ActivationFunctionType
AXX = mybir.AxisListType.X

P = 128
T = 512
D = 1024
NT = T // P
NK = D // P
H = 4
HD = 128
DH = H * HD
NE = 32
TOPK = 4
BT = 32
NBMAX = T * TOPK // BT + NE
NROW = (T + BT) * H
QC = D // H
LIMIT = 7.0
ALPHA = 1.702
EPS = 1e-6
BIG = 3.0e38


def hybrid_layer(nc, x, norm1_gain, w_in, conv_qk, b_igate, b_fgate, mlstm_norm_gain, gmlp_ln_gain,
                 w_spatial, b_spatial, gmlp_out_gain, w_out, norm2_gain, w_router, b_router,
                 w_up, b_up, w_down, b_down, final_gain, out):
    ctx = ExitStack()
    with ctx:
        def sb(name, shape, dt=f32):
            return ctx.enter_context(nc.sbuf_tensor(name, shape, dt))

        def sem(name):
            return ctx.enter_context(nc.semaphore(name))

        def sems(name, n):
            return [sem(f"{name}{i}") for i in range(n)]

        hres = nc.dram_tensor("hres", (NROW, QC), f32, kind="Internal").ap()
        hsrow = nc.dram_tensor("hsrow", (NROW, QC), f32, kind="Internal").ap()

        WSZ = 24576
        W = [sb("W0", [P, WSZ]), sb("W1", [P, WSZ])]
        UPH = NK * 2 * 512

        def up_half(par, h):
            return W[par][:, UPH * h:UPH * (h + 1)].rearrange("p (k g c) -> p k g c", k=NK, g=2)

        def down(par):
            return W[par][:, 2 * UPH:3 * UPH].rearrange("p (k n) -> p k n", k=NK)

        ident = sb("ident", [P, P])
        n2g = sb("n2g", [P, NK])
        idx_tab = sb("idx_tab", [P, NBMAX], u32)
        gate_tab = sb("gate_tab", [P, NBMAX])
        base_tab = sb("base_tab", [P, NE + 2], i32)
        idx_g = sb("idx_g", [P, 1], u32)
        idx_s = sb("idx_s", [P, 1], u32)
        spare = sb("spare", [P, 1])
        half = sb("half", [P, H])
        misc = sb("misc", [P, 3640])
        off = [0]

        def m(n):
            off[0] += n
            return misc[:, off[0] - n:off[0]]

        xg, xT, ysb = m(QC), m(QC), m(QC)
        z = [m(256), m(256)]
        sg = [m(128), m(128)]
        aT = [m(128), m(128)]
        bias_up = [m(512), m(512)]
        bias_dn = [m(QC), m(QC)]
        off[0] = 0
        vaug = m(NT * H * 129).rearrange("p (c h d) -> p c h d", c=NT, h=H)
        wspT = m(DH)
        lng = m(DH)
        tri, maskneg = m(P), m(P)
        rowsT = m(60)
        bg = m(8)
        gf = m(32).rearrange("p (c n) -> p c n", c=NT)
        gtmp = m(16).rearrange("p (c h) -> p c h", c=NT)
        lf = m(16)
        rtok = m(16)
        tq = m(64).rearrange("p (q c h) -> p q c h", q=4, c=NT)
        st = m(64)

        R = W[1]
        xnT = R[:, 0:4096].rearrange("p (k t) -> p k t", k=NK)
        HT = R[:, 0:2048].rearrange("p (b k t) -> p b k t", b=2, k=NK)
        HS = R[:, 2048:4096].rearrange("p (b n) -> p b n", b=2)
        qkpre = R[:, 4096:8216].rearrange("p (f t) -> p f t", f=8)
        WT = R[:, 4096:6144].rearrange("p (c n) -> p c n", c=NT)
        kw = R[:, 6144:7680].rearrange("p (c n) -> p c n", c=3)
        logits = R[:, 7680:7808].rearrange("p (c n) -> p c n", c=NT)
        qkT = R[:, 8216:12312].rearrange("p (f t) -> p f t", f=8)
        osig = R[:, 12312:14360].rearrange("p (c n) -> p c n", c=NT)
        sigtmp = R[:, 12312:13336].rearrange("p (b n) -> p b n", b=2)
        ug = R[:, 14360:16408].rearrange("p (c n) -> p c n", c=NT)
        vg = R[:, 16408:18456].rearrange("p (c n) -> p c n", c=NT)
        G = R[:, 18456:24576]
        xin = G[:, 0:4096].rearrange("p (c n) -> p c n", c=NT)
        cm = [G[0:H, 768 * i:768 * (i + 1)].rearrange("p (c t) -> p c t", c=NT) for i in range(2)]
        Q = G[0:H, 1536:3584].rearrange("p (q c t) -> p q c t", q=4, c=NT)
        bT = G[0:H, 3584:4096].rearrange("p (c t) -> p c t", c=NT)
        mp = G[0:H, 4096:4101]
        Ml = G[0:H, 4104:4108]
        AT = G[:, 0:1024].rearrange("p (b n) -> p b n", b=2)
        ND = G[:, 1024:1540].rearrange("p (h d) -> p h d", h=H)
        Cst = G[:, 1540:2056].rearrange("p (h d) -> p h d", h=H)
        hnT = G[:, 2572:4620].rearrange("p (b k t) -> p b k t", b=2, k=NK)
        negM = G[0:H, 4620:5132].rearrange("p (c t) -> p c t", c=NT)
        wr = G[:, 5136:5392].rearrange("p (k n) -> p k n", k=NK)
        rb = G[:, 5392:5424]
        wg = G[:, 5424:5488].rearrange("p (k n) -> p k n", k=NK)
        sel = G[0:H, 5608:6120].rearrange("p (h t) -> p h t", h=H)

        grp = [W[0][:, 4096 * i:4096 * (i + 1)].rearrange("p (k n) -> p k n", k=NK) for i in range(6)]
        QG, KG, VG, VGG, UG, OG = 4, 5, 0, 1, 2, 3
        wo = W[0][:, 2 * UPH:3 * UPH].rearrange("p (k n) -> p k n", k=NK)
        S = W[0][:, UPH:2 * UPH]
        xres = S[:, 0:4096].rearrange("p (c n) -> p c n", c=NT)
        hcat = S[:, 4096:8192].rearrange("p (c n) -> p c n", c=NT)
        vsqj = G[:, 2056:2568]
        sq1k = R[:, 16408:17432]
        wsp_src = ug[:, 0, :].rearrange("p (g s) -> p g s", g=H)
        rows_src = ug[0:60, 1, 0:P]
        st_f = W[0][:, 9216:9220]

        off[0] = 8216

        def r(n):
            off[0] += n
            return R[:, off[0] - n:off[0]]

        v8 = r(32).rearrange("p (c n) -> p c n", c=NT)
        i8 = r(32).bitcast(u32).rearrange("p (c n) -> p c n", c=NT)
        idxf = r(16).rearrange("p (c k) -> p c k", c=NT)
        gate = r(16).rearrange("p (c k) -> p c k", c=NT)
        gsum = r(4)
        grec = r(4)
        OH = r(512).rearrange("p (c k e) -> p c k e", c=NT, k=TOPK)
        OHD = r(512).rearrange("p (c k e) -> p c k e", c=NT, k=TOPK)
        Mk = r(128).rearrange("p (c e) -> p c e", c=NT)
        pos = r(128).rearrange("p (c e) -> p c e", c=NT)
        iota_i = r(96).bitcast(i32)
        iota_f = r(96)
        tokm_i = r(4).bitcast(i32)
        tokm = r(4)
        part_i = r(4).bitcast(i32)
        partf = r(4)
        ones = r(128)
        stri = r(128)
        tre = r(36)
        cnt = r(8)
        cnt_i = cnt.bitcast(i32)
        nbb = r(128)
        bbs = r(36)
        dest = r(16)
        lo, hi = r(16), r(16)
        Ue = r(2048).rearrange("p (a j t) -> p a j t", a=16, j=H)
        Gv = r(3072).rearrange("p (a w g) -> p a w g", a=16, w=2)
        rowf = r(96)
        zrow = r(256)

        B = [ctx.enter_context(nc.psum_tensor(f"B{i}", [P, 512], f32)) for i in range(8)]

        s_tile = sems("s_tile", NT)
        s_rows, s_wg, s_small, s_late = sem("s_rows"), sem("s_wg"), sem("s_small"), sem("s_late")
        s_grp = sems("s_grp", 6)
        s_wo, s_xres = sem("s_wo"), sem("s_xres")
        s_const = sem("s_const")
        s_xsq, s_xs, s_xT, s_xTe = sem("s_xsq"), sem("s_xs"), sem("s_xT"), sem("s_xTe")
        s_rT, s_rTe = sem("s_rT"), sem("s_rTe")
        s_gates, s_gneg, s_gln, s_lf = sem("s_gates"), sem("s_gneg"), sem("s_gln"), sem("s_lf")
        s_btok, s_rtok, s_rbT, s_q, s_tq, s_tqe = (sem("s_btok"), sem("s_rtok"), sem("s_rbT"), sem("s_q"),
                                                  sem("s_tq"), sem("s_tqe"))
        s_proj, s_pev = sem("s_proj"), sem("s_pev")
        s_conv, s_sig, s_qk = sem("s_conv"), sem("s_sig"), sem("s_qk")
        s_vnm, s_vsq, s_vh = sem("s_vnm"), sem("s_vsq"), sem("s_vh")
        s_wspT, s_wspe, s_wspm = sem("s_wspT"), sem("s_wspe"), sem("s_wspm")
        s_sp, s_hg, s_hsq, s_hgr = sem("s_sp"), sem("s_hg"), sem("s_hsq"), sem("s_hgr")
        s_nm, s_s, s_k = sem("s_nm"), sem("s_s"), sem("s_k")
        s_at, s_e, s_wt, s_kw = sem("s_at"), sem("s_e"), sem("s_wt"), sem("s_kw")
        s_p, s_nd = sem("s_p"), sem("s_nd")
        s_xc, s_lsq, s_hm = sem("s_xc"), sem("s_lsq"), sem("s_hm")
        s_hT, s_hTe, s_out, s_h, s_h2, s_hs = (sem("s_hT"), sem("s_hTe"), sem("s_out"), sem("s_h"), sem("s_h2"),
                                              sem("s_hs"))
        s_nT, s_nTe, s_lg, s_lge = sem("s_nT"), sem("s_nTe"), sem("s_lg"), sem("s_lge")
        s_rowst = sems("s_rowst", NT)
        s_trash = sem("s_trash")
        s_z = sem("s_z")
        s_rc, s_v8, s_ex = sem("s_rc"), sem("s_v8"), sem("s_ex")
        s_mk, s_cnt, s_nbb, s_bb, s_ug, s_tabs, s_tab = (sem("s_mk"), sem("s_cnt"), sem("s_nbb"), sem("s_bb"),
                                                                sem("s_ug"), sem("s_tabs"), sem("s_tab"))
        s_w = [[sems(f"s_w{par}_{third}_", 4) for third in range(3)] for par in range(2)]
        s_bias = sems("s_bias", 2)
        s_eused, s_bused = sem("s_eused"), sem("s_bused")
        m_xg, m_xp, m_xT = sem("m_xg"), sem("m_xp"), sem("m_xT")
        m_u = sems("m_u", 2)
        m_z, m_gl, m_sg, m_lc, m_t, m_act = (sems(n, 2) for n in ("m_z", "m_gl", "m_sg", "m_lc", "m_t", "m_act"))
        m_A, m_aT = sems("m_A", 2), sems("m_aT", 2)
        m_y, m_yb, m_ys, m_sc, m_is, m_ig = sem("m_y"), sem("m_yb"), sem("m_ys"), sem("m_sc"), sem("m_is"), sem("m_ig")
        m_sd = sem("m_sd")
        f_sq, f_out = sem("f_sq"), sem("f_out")
        f_ready, f_y, f_r = sem("f_ready"), sem("f_y"), sem("f_r")
        s_xr, s_vr, s_hsr, s_lr, s_hr = sem("s_xr"), sem("s_vr"), sem("s_hsr"), sem("s_lr"), sem("s_hr")
        ch = {n: sem(f"chain_{n}") for n in ("dve", "pool", "act")}

        def chained(eng, name):
            n = [0]

            def link(ins):
                n[0] += 1
                ins.then_inc(ch[name], 1)
                eng.wait_ge(ch[name], n[0])
            return link

        def wcols(c0):
            return w_in[0, :, c0:c0 + 512].rearrange("(k p) n -> p k n", p=P)

        def load_up(eng, par, h, e, part):
            g, ks = part // 2, slice(4 * (part % 2), 4 * (part % 2) + 4)
            src = w_up[0, e].rearrange("e (k p) (g h c) -> (e p) g h k c", p=P, g=2, h=2)
            eng.dma_start(up_half(par, h)[:, ks, g, :], src[:, g, h, ks]).then_inc(s_w[par][h][part], 16)

        def load_down(eng, par, e, part):
            ks = slice(2 * part, 2 * part + 2)
            src = w_down[0, e].rearrange("e (k p) n -> (e p) k n", p=P)
            eng.dma_start(down(par)[:, ks, :], src[:, ks]).then_inc(s_w[par][2][part], 16)

        NPART = 4
        AHEAD = 3

        def load_all(eng, par, h_or_down, e):
            for part in range(NPART):
                load_down(eng, par, e, part) if h_or_down == 2 else load_up(eng, par, h_or_down, e, part)

        def load_bias(eng, par, e):
            up = b_up[0, e].rearrange("e (a j c) -> (e j) a c", j=H, c=128)
            dn = b_down[0, e].rearrange("e (j c) -> (e j) c", j=H)
            for j in range(H):
                eng.dma_start(bias_up[par][BT * j:BT * (j + 1), :].rearrange("p (a c) -> p a c", c=128),
                              up[j:j + 1].broadcast_to([BT, 4, 128])).then_inc(s_bias[par], 16)
                eng.dma_start(bias_dn[par][BT * j:BT * (j + 1), :],
                              dn[j:j + 1].broadcast_to([BT, QC])).then_inc(s_bias[par], 16)
        NBIAS = 2 * H * 16

        block = ctx.enter_context(nc.Block())

        @block.sync
        def _(sp):
            for c in range(NT):
                sp.dma_start(xin[:, c, :], x[0, P * c:P * (c + 1), :]).then_inc(s_tile[c], 16)
            for slot, c0 in ((QG, 0), (KG, 512), (VG, 1024), (OG, 1536), (VGG, 2568), (UG, 2056)):
                sp.dma_start(grp[slot], wcols(c0)).then_inc(s_grp[slot], 16)
            sp.wait_ge(s_proj, 8)
            sp.dma_start(wo, w_out[0].rearrange("(k p) n -> p k n", p=P)).then_inc(s_wo, 16)
            sp.wait_ge(s_proj, 24)
            for c in range(NT):
                sp.dma_start(xres[:, c, :], x[0, P * c:P * (c + 1), :]).then_inc(s_xres, 16)
            load_all(sp, 0, 0, slice(0, 1))
            for c in range(NT):
                sp.wait_ge(s_hs, c + 1)
                rows = slice(P * H * c, P * H * (c + 1))
                sp.dma_start(hres[rows, :].rearrange("(p j) n -> p (j n)", j=H), xres[:, c, :]).then_inc(s_rowst[c], 16)
                sp.dma_start(hsrow[rows, :].rearrange("(p j) n -> p (j n)", j=H), HS[:, c % 2, :])\
                    .then_inc(s_rowst[c], 16)
            sp.wait_ge(s_out, 2 * NT)
            load_all(sp, 0, 2, slice(0, 1))
            sp.wait_ge(s_lge, NT)
            load_bias(sp, 0, slice(0, 1))
            load_bias(sp, 1, slice(1, 2))
            for c in range(NT):
                sp.wait_ge(s_rowst[c], 32)
            load_all(sp, 0, 1, slice(0, 1))
            load_all(sp, 1, 2, slice(1, 2))
            sp.wait_ge(s_v8, 1)
            load_all(sp, 1, 0, slice(1, 2))
            sp.wait_ge(s_tab, 1)
            sp.wait_ge(s_trash, 32)
            sp.wait_ge(m_xg, 16)
            load_all(sp, 1, 1, slice(1, 2))
            with sp.Fori(1, NE // 2) as i:
                for par in range(2):
                    sp.wait_ge(s_bused, 2 * i + (par - 1))
                    sp.wait_ge(s_eused, 2 * i + (par - 1))
                    e = bass.ts(2 * i + par, 1)
                    for n in range(3 * NPART):
                        third, part = divmod(n, NPART)
                        if n >= AHEAD:
                            t, q = divmod(n - AHEAD, NPART)
                            sp.wait_ge(s_w[par][t][q], 16 * i + 16)
                        load_down(sp, par, e, part) if third == 2 else load_up(sp, par, third, e, part)
                    load_bias(sp, par, e)
            sp.wait_ge(s_eused, NE - 1)
            sp.dma_start(W[0][:, 4096:5120], final_gain.rearrange("(a n) -> a n", a=1).broadcast_to([P, D]))\
                .then_inc(s_late, 16)
            sp.wait_ge(f_ready, 1)
            for c in range(NT):
                rows = slice(P * H * c, P * H * (c + 1))
                sp.dma_start(W[0][:, D * c:D * (c + 1)], hres[rows, :].rearrange("(p j) n -> p (j n)", j=H))\
                    .then_inc(s_tile[c], 16)
            for c in range(NT):
                sp.wait_ge(f_y, c + 1)
                sp.dma_start(out[0, P * c:P * (c + 1), :], W[0][:, D * c:D * (c + 1)]).then_inc(f_out, 16)
            sp.wait_ge(f_out, 16 * NT)

        @block.gpsimd
        def _(pool):
            link = chained(pool, "pool")
            link(pool.memset(half[:], -0.5))
            link(pool.memset(ident[:], 0.0))
            pool.affine_select(out=ident[:], in_=ident[:], compare_op=ALU.not_equal, fill=1.0, base=0,
                               pattern=[[-1, P]], channel_multiplier=1).then_inc(s_const, 1)
            link(pool.memset(tri, 1.0))
            pool.affine_select(out=tri, in_=tri, compare_op=ALU.is_ge, fill=0.0, base=0,
                               pattern=[[1, P]], channel_multiplier=-1).then_inc(s_const, 1)
            link(pool.memset(maskneg, 0.0))
            pool.affine_select(out=maskneg, in_=maskneg, compare_op=ALU.is_ge, fill=-BIG, base=0,
                               pattern=[[1, P]], channel_multiplier=-1).then_inc(s_const, 1)
            link(pool.memset(sel, 0.0))
            pool.affine_select(out=sel, in_=sel, compare_op=ALU.not_equal, fill=1.0, base=0,
                               pattern=[[-1, H], [0, P]], channel_multiplier=1).then_inc(s_const, 1)

            def rstd(col, n, done):
                link(pool.tensor_scalar(col, col, 1.0 / n, EPS, ALU.mult, ALU.add))
                pool.tensor_tensor(col, col, half[:, 0:col.shape[1]], ALU.pow).then_inc(done, 1)

            for c in range(NT):
                pool.wait_ge(s_xsq, c + 1)
                rstd(st[:, c:c + 1], D, s_xr)
            pool.wait_ge(s_wspe, 1)
            pool.affine_select(out=wspT.rearrange("p (g t) -> p g t", g=H), in_=wspT.rearrange("p (g t) -> p g t", g=H),
                               compare_op=ALU.is_ge, fill=0.0, base=0,
                               pattern=[[0, H], [1, P]], channel_multiplier=-1).then_inc(s_wspm, 1)
            def heads(c):
                pool.wait_ge(s_lsq, H * (c + 1))
                rstd(st[:, 24:28], HD, s_lr)

            def gate_in(c):
                pool.wait_ge(s_vsq, c + 1)
                rstd(st[:, 16 + c:17 + c], DH, s_vr)

            def gate_out(c):
                pool.wait_ge(s_hsq, c + 1)
                rstd(st[:, 20 + c:21 + c], DH, s_hsr)

            for step, c in ((heads, 0), (gate_in, 0), (heads, 1), (heads, 2), (gate_in, 1), (heads, 3), (gate_in, 2),
                            (gate_out, 0), (gate_out, 1), (gate_in, 3), (gate_out, 2), (gate_out, 3)):
                step(c)
            pool.wait_ge(s_p, NT * H)
            pool.wait_ge(s_hm, NT)
            pool.wait_ge(s_hgr, NT)
            pool.iota(iota_i, pattern=[[1, NBMAX]], base=0, channel_multiplier=0).then_inc(s_rc, 1)
            pool.iota(tokm_i, pattern=[[P, NT]], base=-T, channel_multiplier=1).then_inc(s_rc, 1)
            pool.iota(part_i[:, 0:1], pattern=[[0, 1]], base=0, channel_multiplier=1).then_inc(s_rc, 1)
            pool.memset(ones, 1.0).then_inc(s_rc, 1)
            pool.memset(zrow, 0.0).then_inc(s_rc, 1)
            link(pool.memset(stri, 1.0))
            pool.affine_select(out=stri, in_=stri, compare_op=ALU.is_gt, fill=0.0, base=0,
                               pattern=[[1, P]], channel_multiplier=-1).then_inc(s_rc, 1)
            link(pool.memset(tre, 1.0))
            pool.affine_select(out=tre, in_=tre, compare_op=ALU.is_gt, fill=0.0, base=0,
                               pattern=[[1, 36]], channel_multiplier=-1).then_inc(s_rc, 1)
            for c in range(NT):
                pool.wait_ge(s_h2, c + 1)
                rstd(st[:, 40 + c:41 + c], D, s_hr)
            pool.wait_ge(s_rc, 7)
            for buf in (hres, hsrow):
                pool.dma_start(buf[T * H:NROW, :], zrow).then_inc(s_trash, 16)
            for c in range(NT):
                pool.wait_ge(s_rowst[c], 32)
            pool.wait_ge(s_trash, 32)
            pool.wait_ge(s_tab, 1)
            total = pool.value_load(base_tab[0:1, NE:NE + 1], min_val=NE, max_val=NBMAX - 1)

            def gather(g):
                pool.tensor_copy(idx_g[:], idx_tab[:, bass.ts(g, 1)]).then_inc(m_ig, 1)
                pool.wait_ge(m_ig, g + 1)
                pool.nop(nofuse=True)
                pool.indirect_dma_start(out=xg, out_offset=None, in_=hsrow,
                                        in_offset=bass.IndirectOffsetOnAxis(ap=idx_g[:, 0:1], axis=0))\
                    .then_inc(m_xg, 16)

            def scatter(g):
                pool.tensor_copy(idx_s[:], idx_tab[:, bass.ts(g, 1)]).then_inc(m_is, 1)
                pool.wait_ge(m_is, g + 1)
                pool.wait_ge(m_ys, g + 1)
                pool.nop(nofuse=True)
                pool.indirect_dma_start(out=hres, out_offset=bass.IndirectOffsetOnAxis(ap=idx_s[:, 0:1], axis=0),
                                        in_=ysb, in_offset=None, compute_op=ALU.add).then_inc(m_sc, 16)

            gather(0)
            pool.wait_ge(m_xp, 1)
            gather(1)
            pool.wait_ge(m_xp, 2)
            gather(2)
            scatter(0)
            with pool.Fori(2, total) as g:
                pool.wait_ge(m_xp, g + 1)
                pool.nop(nofuse=True)
                gather(g + 1)
                pool.wait_ge(m_sc, 16 * (g - 1))
                pool.nop(nofuse=True)
                scatter(g - 1)
            final = pool.value_load(base_tab[0:1, NE + 1:NE + 2], min_val=NE - 1, max_val=NBMAX - 2)
            pool.wait_ge(m_sc, 16 * final)
            pool.nop(nofuse=True)
            scatter(final)
            pool.wait_ge(m_sc, 16 * total)
            pool.nop(nofuse=True)
            pool.wait_ge(m_xg, 16 * total + 16)
            pool.nop(nofuse=True)
            pool.memset(idx_s[:], 0).then_inc(f_ready, 1)
            for c in range(NT):
                pool.wait_ge(f_sq, c + 1)
                rstd(st_f[:, c:c + 1], D, f_r)

        @block.scalar
        def _(act):
            link = chained(act, "act")
            rows = rows_src
            act.dma_start(rows[0:8, :], norm1_gain[0].rearrange("(k p) -> k p", p=P)).then_inc(s_rows, 16)
            act.dma_start(rows[8:12, :], mlstm_norm_gain[0]).then_inc(s_rows, 16)
            act.dma_start(rows[12:16, :], gmlp_out_gain[0].rearrange("(k p) -> k p", p=P)).then_inc(s_rows, 16)
            act.dma_start(rows[16:24, :], norm2_gain[0].rearrange("(k p) -> k p", p=P)).then_inc(s_rows, 16)
            act.dma_start(rows[24:56, :], conv_qk[0].rearrange("j (f p) -> (j f) p", p=P)).then_inc(s_rows, 16)
            act.dma_start(rows[56:60, :], b_spatial[0]).then_inc(s_rows, 16)
            act.dma_start(wg, w_in[0, :, 2048:2056].rearrange("(k p) n -> p k n", p=P)).then_inc(s_wg, 16)
            act.dma_start(bg[:, 0:4], b_igate.broadcast_to([P, H])).then_inc(s_small, 16)
            act.dma_start(bg[:, 4:8], b_fgate.broadcast_to([P, H])).then_inc(s_small, 16)
            act.dma_start(lng, gmlp_ln_gain.broadcast_to([P, DH])).then_inc(s_small, 16)
            act.dma_start(rb, b_router.broadcast_to([P, NE])).then_inc(s_small, 16)
            act.dma_start(wr, w_router[0].rearrange("(k p) n -> p k n", p=P)).then_inc(s_late, 16)
            act.dma_start(wsp_src, w_spatial[0].rearrange("g t s -> t g s")).then_inc(s_late, 16)
            for c in range(NT):
                act.wait_ge(s_tile[c], 16)
                act.activation(qkT[:, 2 * c:2 * c + 2, :], xin[:, c, :].rearrange("p (a n) -> p a n", a=2), ACT.Square,
                               accum_out=st[:, c:c + 1]).then_inc(s_xsq, 1)
            act.wait_ge(s_gneg, 1)
            link(act.activation(gtmp, gtmp, ACT.Exp))
            act.activation(gtmp, gtmp, ACT.Ln, bias=1.0).then_inc(s_gln, 1)
            for n in range(8):
                act.wait_ge(s_proj, n + 1)
                act.activation(qkpre[:, n, 3:515], B[n % 2][:], ACT.Copy).then_inc(s_pev, 1)
                if n >= 1:
                    f = n - 1
                    act.wait_ge(s_conv, f + 1)
                    if f >= 2:
                        act.wait_ge(s_qk, f - 1)
                    act.activation(sigtmp[:, f % 2, :], qkT[:, f, :], ACT.Sigmoid).then_inc(s_sig, 1)
            act.wait_ge(s_conv, 8)
            act.wait_ge(s_qk, 6)
            act.activation(sigtmp[:, 1, :], qkT[:, 7, :], ACT.Sigmoid).then_inc(s_sig, 1)
            for c in range(NT):
                act.wait_ge(s_proj, 9 + c)
                act.activation(vaug[:, c, :, 0:HD], B[c % 2][:].rearrange("p (h d) -> p h d", h=H), ACT.Copy)\
                    .then_inc(s_pev, 1)
            act.wait_ge(s_tq, 1)
            act.activation(tq, B[5][:, 0:64].rearrange("p (q c h) -> p q c h", q=4, c=NT), ACT.Exp).then_inc(s_tqe, 1)
            act.wait_ge(s_qk, 8)
            act.wait_ge(s_tqe, 1)

            def sigmoid_o(c):
                act.wait_ge(s_proj, 13 + c)
                act.activation(osig[:, c, :], B[c % 2][:], ACT.Sigmoid).then_inc(s_pev, 1)

            def gelu_vg(c):
                act.wait_ge(s_proj, 17 + 2 * c)
                act.activation(vg[:, c, :], B[0][:], ACT.Gelu_apprx_tanh, accum_out=st[:, 8 + c:9 + c])\
                    .then_inc(s_pev, 1)

            def gelu_u(c):
                act.wait_ge(s_proj, 18 + 2 * c)
                act.activation(ug[:, c, :], B[1][:], ACT.Gelu_apprx_tanh).then_inc(s_pev, 1)

            def after_squares():
                if squares[0]:
                    act.wait_ge(*squares[0])

            squares = [None]

            def squares_vg(c):
                act.wait_ge(s_vnm, c + 1)
                after_squares()
                act.activation(vsqj, vg[:, c, :], ACT.Square, bias=st[:, 12 + c:13 + c],
                               accum_out=st[:, 16 + c:17 + c]).then_inc(s_vsq, 1)
                squares[0] = (s_vsq, c + 1)

            def squares_gating(c):
                act.wait_ge(s_hg, c + 1)
                after_squares()
                act.activation(vsqj, hcat[:, c, DH:D], ACT.Square, accum_out=st[:, 20 + c:21 + c]).then_inc(s_hsq, 1)
                squares[0] = (s_hsq, c + 1)

            def exps(c):
                act.wait_ge(s_at, c + 1)
                act.activation(AT[:, c % 2, :], AT[:, c % 2, :], ACT.Exp).then_inc(s_e, 1)
                if c < NT - 1:
                    act.wait_ge(s_k, c + 1)
                    for h in range(H):
                        act.activation(kw[:, c, HD * h:HD * (h + 1)], B[4][:, HD * h:HD * (h + 1)], ACT.Copy,
                                       scale=tq[:, 1, c, h:h + 1]).then_inc(s_kw, 1)

            def squares_heads(c):
                act.wait_ge(s_xc, c + 1)
                after_squares()
                for h in range(H):
                    act.activation(vsqj[:, HD * h:HD * (h + 1)], hcat[:, c, HD * h:HD * (h + 1)], ACT.Square,
                                   accum_out=st[:, 24 + h:25 + h]).then_inc(s_lsq, 1)
                squares[0] = (s_lsq, H * (c + 1))

            def squares_h(c):
                act.wait_ge(s_h, 2 * (c + 1))
                if c >= 1:
                    act.wait_ge(s_h2, c)
                act.activation(sq1k, xres[:, c, :], ACT.Square, accum_out=st[:, 40 + c:41 + c]).then_inc(s_h2, 1)

            for c in range(NT):
                sigmoid_o(c)
                exps(c)
            for step, c in ((gelu_vg, 0), (squares_heads, 0), (squares_vg, 0), (gelu_u, 0), (squares_heads, 1),
                            (gelu_vg, 1), (squares_heads, 2), (squares_vg, 1), (gelu_u, 1), (squares_heads, 3),
                            (gelu_vg, 2), (squares_vg, 2), (squares_gating, 0), (gelu_u, 2), (squares_gating, 1),
                            (gelu_vg, 3), (squares_vg, 3), (squares_gating, 2), (gelu_u, 3), (squares_gating, 3),
                            (squares_h, 0), (squares_h, 1), (squares_h, 2), (squares_h, 3)):
                step(c)
            act.wait_ge(s_v8, 1)
            act.activation(gate, gate, ACT.Exp).then_inc(s_ex, 1)
            act.wait_ge(s_tab, 1)
            total = act.value_load(base_tab[0:1, NE:NE + 1], min_val=NE, max_val=NBMAX - 1)
            with act.Fori(0, total) as g:
                for h in range(2):
                    act.wait_ge(m_gl[h], g + 1)
                    act.activation(sg[h], z[h][:, 0:128], ACT.Sigmoid, scale=ALPHA).then_inc(m_sg[h], 1)
                    act.wait_ge(m_A[h], g + 1)
                    act.activation(aT[h], B[3 + h][:, 0:P], ACT.Copy).then_inc(m_aT[h], 1)
            for c in range(NT):
                act.wait_ge(s_tile[c], 32)
                act.activation(W[0][:, 10240 + D * c:10240 + D * (c + 1)], W[0][:, D * c:D * (c + 1)], ACT.Square,
                               accum_out=st_f[:, c:c + 1]).then_inc(f_sq, 1)

        @block.vector
        def _(dve):
            link = chained(dve, "dve")
            V = nc.vector

            V.memset(qkpre[:, :, 0:3], 0.0)
            link(V.memset(vaug[:, :, :, HD:HD + 1], 1.0))
            for c in range(NT):
                dve.wait_ge(s_xr, c + 1)
                V.tensor_scalar(xin[:, c, :], xin[:, c, :], st[:, c:c + 1], None, ALU.mult).then_inc(s_xs, 1)
                if c == 0:
                    dve.wait_ge(s_rT, 1)
                    V.tensor_copy(rowsT, B[5][:, 0:60]).then_inc(s_rTe, 1)
                    dve.wait_ge(s_rTe, 1)
                    V.tensor_copy(n2g[:], rowsT[:, 16:24])
                for hf in range(2):
                    i = 2 * c + hf
                    dve.wait_ge(s_xT, i + 1)
                    V.tensor_tensor(xnT[:, 4 * hf:4 * hf + 4, P * c:P * (c + 1)],
                                    B[6 + hf][:].rearrange("p (k t) -> p k t", k=4),
                                    rowsT[:, 4 * hf:4 * hf + 4].unsqueeze(2).broadcast_to([P, 4, P]), ALU.mult)\
                        .then_inc(s_xTe, 1)
            dve.wait_ge(s_gates, 1)
            dve.wait_ge(s_small, 64)
            link(V.tensor_tensor(gf, B[4][:, 0:32].rearrange("p (c n) -> p c n", c=NT),
                                 bg.unsqueeze(1).broadcast_to([P, NT, 8]), ALU.add))
            link(V.tensor_scalar(gtmp, gf[:, :, 4:8], -1.0, None, ALU.mult))
            V.tensor_tensor(gtmp, gtmp, gf[:, :, 4:8], ALU.min).then_inc(s_gneg, 1)
            dve.wait_ge(s_gln, 1)
            V.scalar_tensor_tensor(lf.rearrange("p (c h) -> p c h", c=NT), gf[:, :, 4:8], 0.0, gtmp,
                                   ALU.min, ALU.subtract).then_inc(s_lf, 1)

            def conv(f):
                dve.wait_ge(s_pev, f + 1)
                for j in range(4):
                    w = rowsT[:, 24 + 8 * j + f:25 + 8 * j + f]
                    if j == 0:
                        ins = V.tensor_scalar(qkT[:, f, :], qkpre[:, f, 0:T], w, None, ALU.mult)
                    else:
                        ins = V.scalar_tensor_tensor(qkT[:, f, :], qkpre[:, f, j:j + T], w, qkT[:, f, :],
                                                     ALU.mult, ALU.add)
                    if j < 3:
                        link(ins)
                ins.then_inc(s_conv, 1)

            def silu(f):
                dve.wait_ge(s_sig, f + 1)
                V.scalar_tensor_tensor(qkT[:, f, :], qkT[:, f, :], 1.0 if f < 4 else HD ** -0.5,
                                       sigtmp[:, f % 2, :], ALU.mult, ALU.mult).then_inc(s_qk, 1)

            def gates_rows():
                rT = B[5][0:H, :].rearrange("p (c t) -> p c t", c=NT)
                V.memset(cm[0][:, :, 0:64], -BIG)
                V.memset(cm[1][:, :, 0:64], -BIG)
                V.memset(mp[:, 0:1], 0.0)
                dve.wait_ge(s_rbT, 1)
                V.tensor_copy(bT, B[4][0:H, :].rearrange("p (c t) -> p c t", c=NT))
                link(V.tensor_copy(cm[0][:, :, 64:192], rT))
                a, d = 0, 1
                while d < P:
                    link(V.tensor_tensor(cm[1 - a][:, :, 64:192], cm[a][:, :, 64:192], cm[a][:, :, 64 - d:192 - d],
                                         ALU.max))
                    a, d = 1 - a, 2 * d
                for c in range(NT):
                    link(V.tensor_tensor(Ml[:, c:c + 1], mp[:, c:c + 1], cm[a][:, c, 191:192], ALU.max))
                    link(V.tensor_tensor(mp[:, c + 1:c + 2], Ml[:, c:c + 1], bT[:, c, P - 1:P], ALU.add))
                mpb = mp[:, 0:NT].unsqueeze(2).broadcast_to([H, NT, P])
                Mlb = Ml[:, :].unsqueeze(2).broadcast_to([H, NT, P])
                link(V.tensor_tensor(negM, cm[a][:, :, 64:192], mpb, ALU.max))
                link(V.tensor_scalar(negM, negM, -1.0, None, ALU.mult))
                V.tensor_tensor(Q[:, 0], negM, mpb, ALU.add)
                V.tensor_tensor(Q[:, 1], rT, Mlb, ALU.subtract)
                V.tensor_tensor(Q[:, 2], mpb, Mlb, ALU.subtract)
                V.tensor_tensor(Q[:, 3], negM, bT, ALU.subtract).then_inc(s_q, 1)

            for f in range(8):
                if f == 2:
                    dve.wait_ge(s_btok, 1)
                    V.tensor_tensor(rtok.rearrange("p (c h) -> p c h", c=NT), gf[:, :, 0:4],
                                    B[5][:, 0:16].rearrange("p (c h) -> p c h", c=NT), ALU.subtract)\
                        .then_inc(s_rtok, 1)
                if f == 6:
                    gates_rows()
                conv(f)
                if f >= 1:
                    silu(f - 1)
            silu(7)
            dve.wait_ge(s_wspT, 1)
            V.tensor_copy(wspT, B[4][:]).then_inc(s_wspe, 1)
            def vg_mean(c):
                dve.wait_ge(s_pev, 17 + 2 * c)
                V.tensor_scalar(st[:, 12 + c:13 + c], st[:, 8 + c:9 + c], -1.0 / DH, None, ALU.mult).then_inc(s_vnm, 1)

            def vg_norm(c):
                dve.wait_ge(s_vr, c + 1)
                link(V.tensor_scalar(vg[:, c, :], vg[:, c, :], st[:, 12 + c:13 + c], st[:, 16 + c:17 + c],
                                     ALU.add, ALU.mult))
                V.tensor_tensor(vg[:, c, :], vg[:, c, :], lng, ALU.mult).then_inc(s_vh, 1)

            def gating(c):
                dve.wait_ge(s_sp, c + 1)
                dve.wait_ge(s_pev, 18 + 2 * c)
                for g in range(H):
                    ins = V.scalar_tensor_tensor(hcat[:, c, DH + P * g:DH + P * (g + 1)], B[7][:, P * g:P * (g + 1)],
                                                 rowsT[:, 56 + g:57 + g], ug[:, c, P * g:P * (g + 1)], ALU.add, ALU.mult)
                ins.then_inc(s_hg, 1)

            def gating_norm(c):
                dve.wait_ge(s_hsr, c + 1)
                V.tensor_scalar(hcat[:, c, DH:D], hcat[:, c, DH:D], st[:, 20 + c:21 + c], None, ALU.mult)\
                    .then_inc(s_hgr, 1)

            def exponents(c):
                dve.wait_ge(s_nm, c + 1)
                if c >= 2:
                    dve.wait_ge(s_wt, c - 1)
                for h in range(H):
                    ins = V.scalar_tensor_tensor(AT[:, c % 2, P * h:P * (h + 1)], B[2][:, P * h:P * (h + 1)],
                                                 rtok[:, H * c + h:H * c + h + 1], maskneg, ALU.add, ALU.add)
                ins.then_inc(s_at, 1)

            def weights(c):
                dve.wait_ge(s_e, c + 1)
                dve.wait_ge(s_s, c + 1)
                V.tensor_tensor(WT[:, c, :], AT[:, c % 2, :], B[3][:], ALU.mult).then_inc(s_wt, 1)

            def numerators(c):
                if c >= 1:
                    dve.wait_ge(s_hm, c)
                for h in range(H):
                    dve.wait_ge(s_p, H * c + h + 1)
                    b = B[5 + h % 2]
                    if c == 0:
                        V.tensor_copy(Cst[:, h, :], b[:, 258:387])
                        V.tensor_copy(ND[:, h, :], b[:, 0:129]).then_inc(s_nd, 1)
                    else:
                        if c < NT - 1:
                            V.scalar_tensor_tensor(Cst[:, h, :], Cst[:, h, :], tq[:, 2, c, h:h + 1], b[:, 258:387],
                                                   ALU.mult, ALU.add)
                        link(V.tensor_scalar(ND[:, h, :], b[:, 129:258], tq[:, 0, c, h:h + 1], None, ALU.mult))
                        V.tensor_tensor(ND[:, h, :], ND[:, h, :], b[:, 0:129], ALU.add).then_inc(s_nd, 1)
                dve.wait_ge(s_nd, H * (c + 1))

            def heads_norm(c):
                den, neg = st[:, 28:32], st[:, 32:36]
                hc = hcat[:, c, 0:DH].rearrange("p (h d) -> p h d", h=H)
                link(V.scalar_tensor_tensor(den, ND[:, :, HD], -1.0, ND[:, :, HD], ALU.mult, ALU.max))
                link(V.tensor_tensor(den, den, tq[:, 3, c, :], ALU.max))
                link(V.reciprocal(den, den))
                link(V.tensor_tensor(hc, ND[:, :, 0:HD], den.unsqueeze(2).broadcast_to([P, H, HD]), ALU.mult))
                link(V.tensor_reduce(neg, hc, AXX, ALU.add))
                link(V.tensor_scalar(neg, neg, -1.0 / HD, None, ALU.mult))
                V.tensor_tensor(hc, hc, neg.unsqueeze(2).broadcast_to([P, H, HD]), ALU.add).then_inc(s_xc, 1)
                dve.wait_ge(s_xc, c + 1)

            def heads_gate(c):
                dve.wait_ge(s_lr, c + 1)
                for h in range(H):
                    s = slice(HD * h, HD * (h + 1))
                    ins = V.scalar_tensor_tensor(hcat[:, c, s], hcat[:, c, s], st[:, 24 + h:25 + h], osig[:, c, s],
                                                 ALU.mult, ALU.mult)
                ins.then_inc(s_hm, 1)

            def cat_evac(c):
                for hf in range(2):
                    dve.wait_ge(s_hT, 2 * c + hf + 1)
                    V.tensor_tensor(HT[:, c % 2, 4 * hf:4 * hf + 4, :], B[2 + hf][:].rearrange("p (k t) -> p k t", k=4),
                                    rowsT[:, 8 + 4 * hf:12 + 4 * hf].unsqueeze(2).broadcast_to([P, 4, P]), ALU.mult)\
                        .then_inc(s_hTe, 1)

            def residual(c):
                for n in range(2):
                    dve.wait_ge(s_out, 2 * c + n + 1)
                    if c == 0 and n == 0:
                        dve.wait_ge(s_xres, 16 * NT)
                    s = slice(512 * n, 512 * (n + 1))
                    V.tensor_tensor(xres[:, c, s], B[n][:], xres[:, c, s], ALU.add).then_inc(s_h, 1)

            def second_norm(c):
                dve.wait_ge(s_hr, c + 1)
                if c >= 2:
                    dve.wait_ge(s_rowst[c - 2], 32)
                    dve.wait_ge(s_nT, 2 * (c - 1))
                V.tensor_scalar(HS[:, c % 2, :], xres[:, c, :], st[:, 40 + c:41 + c], None, ALU.mult).then_inc(s_hs, 1)

            def norm_evac(c):
                for hf in range(2):
                    dve.wait_ge(s_nT, 2 * c + hf + 1)
                    V.tensor_tensor(hnT[:, c % 2, 4 * hf:4 * hf + 4, :], B[4 + hf][:].rearrange("p (k t) -> p k t", k=4),
                                    n2g[:, 4 * hf:4 * hf + 4].unsqueeze(2).broadcast_to([P, 4, P]), ALU.mult)\
                        .then_inc(s_nTe, 1)
                dve.wait_ge(s_lg, c + 1)
                V.tensor_tensor(logits[:, c, :], B[6][:, 0:NE], rb, ALU.add).then_inc(s_lge, 1)

            def heads(c):
                numerators(c)
                heads_norm(c)

            for c in range(NT):
                exponents(c)
                weights(c)
            dve.wait_ge(s_tqe, 1)
            for step, c in ((heads, 0), (vg_mean, 0), (heads_gate, 0), (heads, 1), (heads_gate, 1), (vg_norm, 0),
                            (heads, 2), (vg_mean, 1), (heads_gate, 2), (heads, 3), (vg_norm, 1), (heads_gate, 3),
                            (vg_mean, 2), (gating, 0), (vg_norm, 2), (gating, 1), (gating_norm, 0), (vg_mean, 3),
                            (gating, 2), (vg_norm, 3), (gating_norm, 1), (gating, 3), (gating_norm, 2),
                            (gating_norm, 3), (cat_evac, 0), (cat_evac, 1)):
                step(c)
            for c in range(NT):
                residual(c)
                if c + 2 < NT:
                    cat_evac(c + 2)
                if c >= 1:
                    norm_evac(c - 1)
                second_norm(c)
            norm_evac(NT - 1)

            dve.wait_ge(s_rc, 7)
            dve.wait_ge(s_lge, NT)
            for c in range(NT):
                link(V.max(v8[:, c, :], logits[:, c, :]))
                link(V.max_index(i8[:, c, :], v8[:, c, :], logits[:, c, :]))
            V.tensor_tensor(gate, v8[:, :, 0:TOPK], v8[:, :, 0:1].broadcast_to([P, NT, TOPK]), ALU.subtract)\
                .then_inc(s_v8, 1)
            V.tensor_copy(idxf, i8[:, :, 0:TOPK])
            V.tensor_copy(iota_f, iota_i)
            V.tensor_copy(tokm, tokm_i)
            V.tensor_scalar(part_i[:, 1:2], part_i[:, 0:1], 5, None, ALU.logical_shift_right)
            link(V.tensor_scalar(part_i[:, 2:3], part_i[:, 0:1], 31, None, ALU.bitwise_and))
            link(V.tensor_copy(partf[:, 1:3], part_i[:, 1:3]))
            V.tensor_scalar(partf[:, 3:4], partf[:, 1:2], float(T * H), None, ALU.add)
            link(V.tensor_tensor(OH, iota_f[:, 0:NE].unsqueeze(1).unsqueeze(1).broadcast_to([P, NT, TOPK, NE]),
                                 idxf.unsqueeze(3).broadcast_to([P, NT, TOPK, NE]), ALU.is_equal))
            V.tensor_reduce(Mk, OH.rearrange("p c k e -> p c e k"), AXX, ALU.add).then_inc(s_mk, 1)
            dve.wait_ge(s_ex, 1)
            link(V.tensor_reduce(gsum, gate, AXX, ALU.add))
            link(V.reciprocal(grec, gsum))
            link(V.tensor_tensor(gate, gate, grec.unsqueeze(2).broadcast_to([P, NT, TOPK]), ALU.mult))
            dve.wait_ge(s_cnt, 1)
            link(V.tensor_scalar(cnt[0:NE, 0:1], B[0][0:NE, 0:1], float(BT - 1), None, ALU.add))
            link(V.tensor_copy(cnt_i[0:NE, 1:2], cnt[0:NE, 0:1]))
            link(V.tensor_scalar(cnt_i[0:NE, 2:3], cnt_i[0:NE, 1:2], 5, None, ALU.logical_shift_right))
            link(V.tensor_copy(cnt[0:NE, 3:4], cnt_i[0:NE, 2:3]))
            link(V.tensor_scalar(cnt[0:NE, 4:5], cnt[0:NE, 3:4], 1.0, None, ALU.max))
            V.tensor_scalar(nbb[0:NE, :], ones[0:NE, :], cnt[0:NE, 4:5], None, ALU.mult).then_inc(s_nbb, 1)
            dve.wait_ge(s_bb, 1)
            link(V.tensor_scalar(bbs[:, 0:NE + 1], B[1][:, 0:NE + 1], 1.0, None, ALU.mult))
            link(V.tensor_scalar(bbs[:, NE + 1:NE + 2], bbs[:, NE:NE + 1], -1.0, None, ALU.add))
            V.tensor_copy(base_tab[:], bbs[:, 0:NE + 2])
            link(V.scalar_tensor_tensor(pos, bbs[:, 0:NE].unsqueeze(1).broadcast_to([P, NT, NE]), float(BT),
                                        B[2][:, 0:128].rearrange("p (c e) -> p c e", c=NT), ALU.mult, ALU.add))
            link(V.tensor_tensor(OHD, OH, pos.unsqueeze(2).broadcast_to([P, NT, TOPK, NE]), ALU.mult))
            link(V.tensor_reduce(dest, OHD, AXX, ALU.add))
            desti = lo.bitcast(i32)
            link(V.tensor_copy(desti, dest))
            hii = hi.bitcast(i32)
            link(V.tensor_scalar(hii, desti, 5, None, ALU.logical_shift_right))
            link(V.tensor_scalar(desti, desti, 31, None, ALU.bitwise_and))
            link(V.tensor_copy(hi, hii))
            link(V.tensor_copy(lo, desti))
            V.tensor_tensor(Ue, iota_f[:, 0:BT].unsqueeze(1).unsqueeze(1).broadcast_to([P, 16, H, BT]),
                            lo.unsqueeze(2).unsqueeze(3).broadcast_to([P, 16, H, BT]), ALU.is_equal)
            link(V.tensor_tensor(Gv[:, :, 1, :], iota_f.unsqueeze(1).broadcast_to([P, 16, NBMAX]),
                                 hi.unsqueeze(2).broadcast_to([P, 16, NBMAX]), ALU.is_equal))
            link(V.tensor_tensor(Gv[:, :, 0, :].rearrange("p (c k) g -> p c k g", c=NT),
                                 Gv[:, :, 1, :].rearrange("p (c k) g -> p c k g", c=NT),
                                 tokm.unsqueeze(2).unsqueeze(3).broadcast_to([P, NT, TOPK, NBMAX]), ALU.mult))
            V.tensor_tensor(Gv[:, :, 1, :].rearrange("p (c k) g -> p c k g", c=NT),
                            Gv[:, :, 1, :].rearrange("p (c k) g -> p c k g", c=NT),
                            gate.unsqueeze(3).broadcast_to([P, NT, TOPK, NBMAX]), ALU.mult).then_inc(s_ug, 1)
            dve.wait_ge(s_tabs, 1)
            V.tensor_copy(gate_tab[:], B[3][:, NBMAX:2 * NBMAX])
            link(V.tensor_scalar(rowf, B[3][:, 0:NBMAX], 0.0, partf[:, 2:3], ALU.is_equal, ALU.mult))
            link(V.scalar_tensor_tensor(rowf, rowf, 1.0, B[3][:, 0:NBMAX], ALU.mult, ALU.add))
            link(V.tensor_scalar(rowf, rowf, float(H), partf[:, 3:4], ALU.mult, ALU.add))
            V.tensor_copy(idx_tab[:], rowf).then_inc(s_tab, 1)

            def block_steps(g, par):
                bu = bias_up[par].rearrange("p (g h c) -> p g h c", g=2, h=2)
                for h in range(2):
                    dve.wait_ge(m_u[h], g + 1)
                    V.tensor_tensor(z[h].rearrange("p (g c) -> p g c", g=2), B[h][:, 0:256].rearrange("p (g c) -> p g c", g=2),
                                    bu[:, :, h, :], ALU.add).then_inc(m_z[h], 1)
                    dve.wait_ge(m_z[h], g + 1)
                    V.tensor_scalar(z[h][:, 0:128], z[h][:, 0:128], LIMIT, None, ALU.min).then_inc(m_gl[h], 1)
                    V.tensor_scalar(z[h][:, 128:256], z[h][:, 128:256], LIMIT, -LIMIT, ALU.min, ALU.max).then_inc(m_lc[h], 1)
                    dve.wait_ge(m_lc[h], g + 1)
                    V.scalar_tensor_tensor(z[h][:, 128:256], z[h][:, 128:256], 1.0, z[h][:, 0:128], ALU.add, ALU.mult)\
                        .then_inc(m_t[h], 1)
                    dve.wait_ge(m_t[h], g + 1)
                    dve.wait_ge(m_sg[h], g + 1)
                    V.tensor_tensor(z[h][:, 128:256], z[h][:, 128:256], sg[h], ALU.mult).then_inc(m_act[h], 1)
                x_evac(g + 1)
                dve.wait_ge(m_y, g + 1)
                dve.wait_ge(m_is, g + 1)
                V.tensor_tensor(ysb, B[5][:, 0:QC], bias_dn[par], ALU.add).then_inc(m_yb, 1)
                dve.wait_ge(m_yb, g + 1)
                V.tensor_scalar(ysb, ysb, gate_tab[:, bass.ts(g, 1)], None, ALU.mult).then_inc(m_ys, 1)

            def x_evac(g):
                dve.wait_ge(m_xp, g + 1)
                V.tensor_tensor(xT.rearrange("p (h j t) -> p h j t", h=2, j=H), B[2][:, 0:256].rearrange("p (h j t) -> p h j t", h=2, j=H),
                                n2g[:].rearrange("p (j h) -> p h j", h=2).unsqueeze(3).broadcast_to([P, 2, H, BT]), ALU.mult)\
                    .then_inc(m_xT, 1)

            dve.wait_ge(s_tab, 1)
            x_evac(0)
            with dve.Fori(0, NE // 2) as i:
                for par in range(2):
                    first = dve.value_load(base_tab[0:1, bass.ts(2 * i + par, 1)], min_val=0, max_val=NBMAX - 2)
                    last = dve.value_load(base_tab[0:1, bass.ts(2 * i + par + 1, 1)], min_val=1, max_val=NBMAX - 1)
                    with dve.Fori(first, last) as g:
                        dve.wait_ge(s_bias[par], NBIAS * i + NBIAS)
                        block_steps(g, par)
                    V.memset(spare[:], 0.0).then_inc(s_bused, 1)
            dve.wait_ge(s_late, 48)
            for c in range(NT):
                dve.wait_ge(f_r, c + 1)
                tile = W[0][:, D * c:D * (c + 1)]
                V.scalar_tensor_tensor(tile, tile, st_f[:, c:c + 1], W[0][:, 4096:5120], ALU.mult, ALU.mult)\
                    .then_inc(f_y, 1)

        @block.tensor
        def _(pe):
            mm = nc.tensor.matmul

            def project(n, lhs, rhs, slot):
                pe.wait_ge(s_grp[slot], 16)
                if n >= 2:
                    pe.wait_ge(s_pev, n - 1)
                for k in range(NK):
                    ins = mm(B[n % 2][:], lhs(k), rhs(k), start=(k == 0), stop=(k == NK - 1))
                ins.then_inc(s_proj, 1)

            def tokens(n, c, slot):
                project(n, lambda k: xnT[:, k, P * c:P * (c + 1)], lambda k: grp[slot][:, k, :], slot)

            pe.wait_ge(s_const, 1)
            pe.wait_ge(s_rows, 96)
            nc.tensor.transpose(B[5][:, 0:60], rows_src, ident[0:60, 0:60]).then_inc(s_rT, 1)
            for c in range(NT):
                pe.wait_ge(s_xs, c + 1)
                for hf in range(2):
                    if c >= 1:
                        pe.wait_ge(s_xTe, 2 * c + hf - 1)
                    for k in range(4):
                        ins = nc.tensor.transpose(B[6 + hf][:, P * k:P * (k + 1)],
                                                  xin[:, c, P * (4 * hf + k):P * (4 * hf + k + 1)], ident[:])
                    ins.then_inc(s_xT, 1)
            pe.wait_ge(s_wg, 16)
            pe.wait_ge(s_xTe, 2 * NT)
            for c in range(NT):
                for k in range(NK):
                    ins = mm(B[4][:, 8 * c:8 * (c + 1)], xnT[:, k, P * c:P * (c + 1)], wg[:, k, :],
                             start=(k == 0), stop=(k == NK - 1))
            ins.then_inc(s_gates, 1)
            for f in range(8):
                slot, col = (QG, KG)[f // 4], 128 * (f % 4)
                project(f, lambda k: grp[slot][:, k, col:col + 128], lambda k: xnT[:, k, :], slot)
                if f == 1:
                    pe.wait_ge(s_lf, 1)
                    pe.wait_ge(s_const, 4)
                    mm(B[5][:, 0:16], tri, lf, start=True, stop=True).then_inc(s_btok, 1)
                if f == 3:
                    pe.wait_ge(s_rtok, 1)
                    for c in range(NT):
                        mm(B[5][0:H, P * c:P * (c + 1)], rtok[:, H * c:H * (c + 1)], ident[:], start=True, stop=True)
                        ins = mm(B[4][0:H, P * c:P * (c + 1)], lf[:, H * c:H * (c + 1)], tri, start=True, stop=True)
                    ins.then_inc(s_rbT, 1)
            for c in range(NT):
                tokens(8 + c, c, VG)
            pe.wait_ge(s_q, 1)
            for q in range(4):
                for c in range(NT):
                    o = 16 * q + 4 * c
                    ins = mm(B[5][:, o:o + 4], Q[:, q, c, :], ident[0:H, 0:H], start=True, stop=True)
            ins.then_inc(s_tq, 1)
            pe.wait_ge(s_late, 32)
            for g in range(H):
                ins = nc.tensor.transpose(B[4][:, P * g:P * (g + 1)], wsp_src[:, g, :], ident[:])
            ins.then_inc(s_wspT, 1)
            def spatial(c):
                pe.wait_ge(s_vh, c + 1)
                pe.wait_ge(*((s_hg, c) if c >= 1 else (s_wspm, 1)))
                for g in range(H):
                    ins = mm(B[7][:, P * g:P * (g + 1)], wspT[:, P * g:P * (g + 1)], vg[:, c, P * g:P * (g + 1)],
                             start=True, stop=True)
                ins.then_inc(s_sp, 1)

            def chunk_products(c):
                t = slice(P * c, P * (c + 1))
                if c >= 1:
                    pe.wait_ge(s_at, c)
                for h in range(H):
                    ins = mm(B[2][:, P * h:P * (h + 1)], sel[:, h, :], negM[:, c, :], start=True, stop=True)
                ins.then_inc(s_nm, 1)
                if c >= 1:
                    pe.wait_ge(s_wt, c)
                for h in range(H):
                    ins = mm(B[3][:, P * h:P * (h + 1)], qkT[:, H + h, t], qkT[:, h, t], start=True, stop=True)
                ins.then_inc(s_s, 1)
                if c < NT - 1:
                    pe.wait_ge(*((s_kw, H * c) if c >= 1 else (s_wspe, 1)))
                    for h in range(H):
                        ins = nc.tensor.transpose(B[4][:, P * h:P * (h + 1)], qkT[:, H + h, t], ident[:])
                    ins.then_inc(s_k, 1)

            def chunk_heads(c):
                pe.wait_ge(s_wt, c + 1)
                if c < NT - 1:
                    pe.wait_ge(s_kw, H * (c + 1))
                for h in range(H):
                    i = H * c + h
                    if i >= 2:
                        pe.wait_ge(s_nd, i - 1)
                    b = B[5 + h % 2]
                    ins = mm(b[:, 0:129], WT[:, c, P * h:P * (h + 1)], vaug[:, c, h, :], start=True, stop=True)
                    if c >= 1:
                        ins = mm(b[:, 129:258], qkT[:, h, P * c:P * (c + 1)], Cst[:, h, :], start=True, stop=True)
                    if c < NT - 1:
                        ins = mm(b[:, 258:387], kw[:, c, HD * h:HD * (h + 1)], vaug[:, c, h, :], start=True, stop=True)
                    ins.then_inc(s_p, 1)

            def transposes(src, bank, done):
                for hf in range(2):
                    for k in range(4):
                        ins = nc.tensor.transpose(B[bank + hf][:, P * k:P * (k + 1)],
                                                  src[:, P * (4 * hf + k):P * (4 * hf + k + 1)], ident[:])
                    ins.then_inc(done, 1)

            def cat(c):
                pe.wait_ge(s_hm, c + 1)
                pe.wait_ge(s_hgr, c + 1)
                if c >= 1:
                    pe.wait_ge(s_hTe, 2 * c)
                transposes(hcat[:, c, :], 2, s_hT)

            def project_out(c):
                pe.wait_ge(s_hTe, 2 * c + 2)
                for n in range(2):
                    if c >= 1:
                        pe.wait_ge(s_h, 2 * (c - 1) + n + 1)
                    for k in range(NK):
                        ins = mm(B[n][:], HT[:, c % 2, k, :], wo[:, k, 512 * n:512 * (n + 1)],
                                 start=(k == 0), stop=(k == NK - 1))
                    ins.then_inc(s_out, 1)

            def router(c):
                pe.wait_ge(s_hs, c + 1)
                if c >= 1:
                    pe.wait_ge(s_nTe, 2 * c)
                transposes(HS[:, c % 2, :], 4, s_nT)
                pe.wait_ge(s_nTe, 2 * c + 2)
                if c >= 1:
                    pe.wait_ge(s_lge, c)
                for k in range(NK):
                    ins = mm(B[6][:, 0:NE], hnT[:, c % 2, k, :], wr[:, k, :], start=(k == 0), stop=(k == NK - 1))
                ins.then_inc(s_lg, 1)

            pe.wait_ge(s_qk, 8)
            for c in range(NT):
                tokens(12 + c, c, OG)
                chunk_products(c)
            for c in range(NT):
                tokens(16 + 2 * c, c, VGG)
                if c < 2:
                    chunk_heads(2 * c)
                else:
                    spatial(2 * (c - 2))
                tokens(17 + 2 * c, c, UG)
                if c < 2:
                    chunk_heads(2 * c + 1)
                else:
                    spatial(2 * (c - 2) + 1)
            pe.wait_ge(s_pev, 24)
            pe.wait_ge(s_wo, 16)
            cat(0)
            cat(1)
            for c in range(NT):
                project_out(c)
                if c + 2 < NT:
                    cat(c + 2)
                if c >= 1:
                    router(c - 1)
            router(NT - 1)
            pe.wait_ge(s_mk, 1)
            pe.wait_ge(s_rc, 7)
            for c in range(NT):
                mm(B[0][0:NE, 0:1], Mk[:, c, :], ones[:, 0:1], start=(c == 0), stop=(c == NT - 1))
            for c in range(NT):
                for d in range(c + 1):
                    ins = mm(B[2][:, NE * c:NE * (c + 1)], stri if d == c else ones, Mk[:, d, :],
                             start=(d == 0), stop=(d == c))
            ins.then_inc(s_cnt, 1)
            pe.wait_ge(s_nbb, 1)
            mm(B[1][:, 0:NE + 1], nbb[0:NE, :], tre[0:NE, 0:NE + 1], start=True, stop=True).then_inc(s_bb, 1)
            pe.wait_ge(s_ug, 1)
            for a in range(NT * TOPK):
                ins = mm(B[3][:, 0:2 * NBMAX], Ue[:, a].rearrange("p j t -> p (j t)"),
                         Gv[:, a].rearrange("p w g -> p (w g)"), start=(a == 0), stop=(a == NT * TOPK - 1))
            ins.then_inc(s_tabs, 1)

            def transpose_block(g):
                pe.wait_ge(m_xg, 16 * g + 16)
                for h in range(2):
                    ins = nc.tensor.transpose(B[2][:, P * h:P * (h + 1)], xg[:, P * h:P * (h + 1)], ident[:])
                ins.then_inc(m_xp, 1)

            def transpose_act(g, h):
                pe.wait_ge(m_act[h], g + 1)
                nc.tensor.transpose(B[3 + h][:, 0:P], z[h][:, 128:256], ident[:]).then_inc(m_A[h], 1)

            pe.wait_ge(s_tab, 1)
            transpose_block(0)
            with pe.Fori(0, NE // 2) as i:
                for par in range(2):
                    first = pe.value_load(base_tab[0:1, bass.ts(2 * i + par, 1)], min_val=0, max_val=NBMAX - 2)
                    last = pe.value_load(base_tab[0:1, bass.ts(2 * i + par + 1, 1)], min_val=1, max_val=NBMAX - 1)
                    for part in range(NPART):
                        pe.wait_ge(s_w[par][0][part], 16 * i + 16)
                        pe.wait_ge(s_w[par][1][part], 16 * i + 16)
                    pe.nop(nofuse=True)
                    with pe.Fori(first, last) as g:
                        pe.wait_ge(m_xT, g + 1)
                        for h in range(2):
                            w = up_half(par, h)
                            for k in range(NK):
                                if h == 1 and k == 5:
                                    transpose_act(g, 0)
                                o = P * (k % 2) + BT * (k // 2)
                                for j in range(H):
                                    ins = mm(B[h][BT * j:BT * (j + 1), 0:256].rearrange("p (g c) -> p g c", g=2),
                                             xT[:, o:o + BT], w[:, k, :, P * j:P * (j + 1)],
                                             start=(k == 0), stop=(k == NK - 1))
                            ins.then_inc(m_u[h], 1)
                        pe.wait_ge(m_aT[0], g + 1)
                        for part in range(NPART):
                            pe.wait_ge(s_w[par][2][part], 16 * i + 16)
                        for h in range(2):
                            if h == 1:
                                transpose_act(g, 1)
                                transpose_block(g + 1)
                                pe.wait_ge(m_aT[1], g + 1)
                            for q in range(H):
                                for j in range(H):
                                    ins = mm(B[5][BT * j:BT * (j + 1), 0:QC], aT[h][:, BT * q:BT * (q + 1)],
                                             down(par)[:, H * h + q, QC * j:QC * (j + 1)],
                                             start=(h == 0 and q == 0), stop=(h == 1 and q == H - 1))
                        ins.then_inc(m_y, 1)
                    mm(B[6][0:BT, 0:2], ident[:, 0:BT], ident[:, 0:2], start=True, stop=True).then_inc(s_eused, 1)


_INS = ["x", "norm1_gain", "w_in", "conv_qk", "b_igate", "b_fgate", "mlstm_norm_gain", "gmlp_ln_gain",
        "w_spatial", "b_spatial", "gmlp_out_gain", "w_out", "norm2_gain", "w_router", "b_router",
        "w_up", "b_up", "w_down", "b_down", "final_gain"]
_OUTS = [((1, T, D), "float32")]


def kernel(**inputs):
    import numpy as _np
    import concourse.bacc as _bacc
    from concourse import mybir as _mybir
    from concourse.bass_utils import run_bass_kernel_spmd as _run

    nc = _bacc.Bacc("TRN2", target_bir_lowering=False, num_devices=1)
    arrays, args = {}, []
    for name in _INS:
        a = _np.ascontiguousarray(inputs[name])
        arrays[f"in_{name}_dram"] = a
        args.append(nc.dram_tensor(f"in_{name}_dram", a.shape, _mybir.dt.from_np(a.dtype), kind="ExternalInput").ap())
    for i, (shape, dtype) in enumerate(_OUTS):
        dt = _mybir.dt.from_np(_np.dtype(dtype))
        args.append(nc.dram_tensor(f"out_{i}_dram", shape, dt, kind="ExternalOutput").ap())
    hybrid_layer(nc, *args)
    r = _run(nc, [arrays], core_ids=[0])
    return r.results[0]["out_0_dram"]
```

```python
import concourse.bass as bass
from concourse import mybir
from contextlib import ExitStack

f32 = mybir.dt.float32
f16 = mybir.dt.float16
i32 = mybir.dt.int32
u32 = mybir.dt.uint32
ALU = mybir.AluOpType
ACT = mybir.ActivationFunctionType
AXX = mybir.AxisListType.X

P = 128
T = 512
D = 1024
NT = T // P
NK = D // P
H = 4
HD = 128
DH = H * HD
NE = 32
TOPK = 4
BT = 32
NBMAX = T * TOPK // BT + NE
NROW = (T + BT) * H
QC = D // H
LIMIT = 7.0
ALPHA = 1.702
EPS = 1e-6
BIG = 3.0e38


def hybrid_layer(nc, x, norm1_gain, w_in, conv_qk, b_igate, b_fgate, mlstm_norm_gain, gmlp_ln_gain,
                 w_spatial, b_spatial, gmlp_out_gain, w_out, norm2_gain, w_router, b_router,
                 w_up, b_up, w_down, b_down, final_gain, out):
    ctx = ExitStack()
    with ctx:
        def sb(name, shape, dt=f32):
            return ctx.enter_context(nc.sbuf_tensor(name, shape, dt))

        def sem(name):
            return ctx.enter_context(nc.semaphore(name))

        def sems(name, n):
            return [sem(f"{name}{i}") for i in range(n)]

        hres = nc.dram_tensor("hres", (NROW, QC), f32, kind="Internal").ap()
        hsrow = nc.dram_tensor("hsrow", (NROW, QC), f32, kind="Internal").ap()

        WSZ = 24576
        W = [sb("W0", [P, WSZ]), sb("W1", [P, WSZ])]
        UPH = NK * 2 * 512

        def up(par):
            return W[par][:, 0:2 * UPH].rearrange("p (k g h c) -> p k g h c", k=NK, g=2, h=2)

        def down(par):
            return W[par][:, 2 * UPH:3 * UPH].rearrange("p (k n) -> p k n", k=NK)

        ident = sb("ident", [P, P])
        n2g = sb("n2g", [P, NK])
        idx_tab = sb("idx_tab", [P, NBMAX], u32)
        gate_tab = sb("gate_tab", [P, NBMAX + 1])
        order_tab = sb("order_tab", [P, NE], i32)
        base_tab = sb("base_tab", [P, NE + 2], i32)
        idx_g = sb("idx_g", [P, 1], u32)
        idx_s = sb("idx_s", [P, 1], u32)
        half = sb("half", [P, H])
        misc = sb("misc", [P, 3624])
        off = [0]

        def m(n):
            off[0] += n
            return misc[:, off[0] - n:off[0]]

        xg, xT, ysb = m(QC), m(QC), m(QC)
        z = m(512)
        sg, aT = m(256), m(256)
        BIAS0 = off[0]
        bias_all = [m(512 + QC), m(512 + QC)]
        bias_up = [b[:, 0:512] for b in bias_all]
        bias_dn = [b[:, 512:512 + QC] for b in bias_all]
        off[0] = 0
        vaug = m(NT * H * 129).rearrange("p (c h d) -> p c h d", c=NT, h=H)
        wspT = m(DH)
        lng = m(DH)
        tri, maskneg = m(P), m(P)
        rowsT = m(60)
        bg = m(8)
        gf = m(32).rearrange("p (c n) -> p c n", c=NT)
        gtmp = m(16).rearrange("p (c h) -> p c h", c=NT)
        lf = m(16)
        rtok = m(16)
        tq = m(64).rearrange("p (q c h) -> p q c h", q=4, c=NT)
        st = m(64)

        R = W[1]
        xnT = R[:, 0:4096].rearrange("p (k t) -> p k t", k=NK)
        HT = R[:, 0:2048].rearrange("p (b k t) -> p b k t", b=2, k=NK)
        HS = R[:, 2048:4096].rearrange("p (b n) -> p b n", b=2)
        qkpre = R[:, 4096:8216].rearrange("p (f t) -> p f t", f=8)
        WT = R[:, 4096:6144].rearrange("p (c n) -> p c n", c=NT)
        kw = R[:, 6144:7680].rearrange("p (c n) -> p c n", c=3)
        logits = misc[:, 1024:1152].rearrange("p (c n) -> p c n", c=NT)
        qkT = R[:, 8216:12312].rearrange("p (f t) -> p f t", f=8)
        osig = R[:, 12312:14360].rearrange("p (c n) -> p c n", c=NT)
        sigtmp = R[:, 12312:13336].rearrange("p (b n) -> p b n", b=2)
        ug = R[:, 14360:16408].rearrange("p (c n) -> p c n", c=NT)
        vg = R[:, 16408:18456].rearrange("p (c n) -> p c n", c=NT)
        G = R[:, 18456:24576]
        xin = G[:, 0:4096].rearrange("p (c n) -> p c n", c=NT)
        cm = [G[0:H, 768 * i:768 * (i + 1)].rearrange("p (c t) -> p c t", c=NT) for i in range(2)]
        Q = G[0:H, 1536:3584].rearrange("p (q c t) -> p q c t", q=4, c=NT)
        bT = G[0:H, 3584:4096].rearrange("p (c t) -> p c t", c=NT)
        mp = G[0:H, 4096:4101]
        Ml = G[0:H, 4104:4108]
        AT = G[:, 0:1024].rearrange("p (b n) -> p b n", b=2)
        ND = G[:, 1024:1540].rearrange("p (h d) -> p h d", h=H)
        Cst = G[:, 1540:2056].rearrange("p (h d) -> p h d", h=H)
        hnT = G[:, 2572:4620].rearrange("p (b k t) -> p b k t", b=2, k=NK)
        negM = G[0:H, 4620:5132].rearrange("p (c t) -> p c t", c=NT)
        wr = G[:, 5136:5392].rearrange("p (k n) -> p k n", k=NK)
        rb = G[:, 5392:5424]
        wg = G[:, 5424:5488].rearrange("p (k n) -> p k n", k=NK)
        sel = G[0:H, 5608:6120].rearrange("p (h t) -> p h t", h=H)

        grp = [W[0][:, 4096 * i:4096 * (i + 1)].rearrange("p (k n) -> p k n", k=NK) for i in range(6)]
        VG, VGG, QG, KG, UG, OG = range(6)
        wo = W[0][:, UPH:2 * UPH].rearrange("p (k n) -> p k n", k=NK)
        S = W[0][:, 2 * UPH:3 * UPH]
        xres = S[:, 0:4096].rearrange("p (c n) -> p c n", c=NT)
        hcat = S[:, 4096:8192].rearrange("p (c n) -> p c n", c=NT)
        vsqj = G[:, 2056:2568]
        sq1k = misc[:, 0:1024]
        wsp_src = ug[:, 0, :].rearrange("p (g s) -> p g s", g=H)
        rows_src = ug[0:60, 1, 0:P]
        st_f = W[0][:, 9216:9220]

        off[0] = 8216

        def r(n):
            off[0] += n
            return R[:, off[0] - n:off[0]]

        v8 = r(32).rearrange("p (c n) -> p c n", c=NT)
        i8 = r(32).bitcast(u32).rearrange("p (c n) -> p c n", c=NT)
        idxf = r(16).rearrange("p (c k) -> p c k", c=NT)
        gate = r(16).rearrange("p (c k) -> p c k", c=NT)
        gsum = r(4)
        grec = r(4)
        OH = r(512).rearrange("p (c k e) -> p c k e", c=NT, k=TOPK)
        OHD = r(512).rearrange("p (c k e) -> p c k e", c=NT, k=TOPK)
        Mk = r(128).rearrange("p (c e) -> p c e", c=NT)
        pos = r(128).rearrange("p (c e) -> p c e", c=NT)
        iota_i = r(96).bitcast(i32)
        iota_f = r(96)
        tokm_i = r(4).bitcast(i32)
        tokm = r(4)
        part_i = r(4).bitcast(i32)
        partf = r(4)
        ones = r(128)
        stri = r(128)
        tre = r(36)
        cnt = r(8)
        cnt_i = cnt.bitcast(i32)
        nbb = r(128 + NE)
        bbs = r(36)
        expb = r(128)
        late = r(4)
        before = r(36)
        behind, atp = r(36), r(36)
        dest = r(16)
        lo, hi = r(16), r(16)
        Mk16 = r(64).bitcast(f16).rearrange("p (c e) -> p c e", c=NT)
        ones16, stri16 = r(64).bitcast(f16), r(64).bitcast(f16)
        iota16 = r(48).bitcast(f16)
        lo16, hi16 = r(8).bitcast(f16), r(8).bitcast(f16)
        U16 = r(256).bitcast(f16).rearrange("p (a t) -> p a t", a=16)
        UT16 = r(256).bitcast(f16).rearrange("p (a t) -> p a t", a=16)
        G16 = r(768).bitcast(f16).rearrange("p (a g) -> p a g", a=16)
        Ug = r(512).rearrange("p (a t) -> p a t", a=16)
        tok_s, gate_s = r(48).bitcast(f16)[0:BT, :], r(96)[0:BT, :]
        spread16 = r(64).bitcast(f16)[0:BT, :].rearrange("p (j t) -> p j t", j=H)
        spread = r(128)[0:BT, :].rearrange("p (j t) -> p j t", j=H)
        G32 = misc[:, QC:QC + 1536].rearrange("p (a g) -> p a g", a=16)
        rowf = r(96)
        zrow = r(256)

        assert off[0] <= 14336
        B = [ctx.enter_context(nc.psum_tensor(f"B{i}", [P, 512], f32)) for i in range(8)]

        s_tile = sems("s_tile", NT)
        s_late_e, s_before, s_place, s_atp, s_order = (sem("s_late_e"), sem("s_before"), sem("s_place"), sem("s_atp"),
                                                       sem("s_order"))
        s_gb, s_gtab, s_small_tab, s_spread, s_g32 = (sem("s_gb"), sem("s_gtab"), sem("s_small_tab"), sem("s_spread"),
                                                      sem("s_g32"))
        s_rows, s_wg, s_small, s_late = sem("s_rows"), sem("s_wg"), sem("s_small"), sem("s_late")
        s_grp = sems("s_grp", 6)
        s_wo, s_xres = sem("s_wo"), sem("s_xres")
        s_const = sem("s_const")
        s_xsq, s_xs, s_xT, s_xTe = sem("s_xsq"), sem("s_xs"), sem("s_xT"), sem("s_xTe")
        s_rT, s_rTe = sem("s_rT"), sem("s_rTe")
        s_gates, s_gneg, s_gln, s_lf = sem("s_gates"), sem("s_gneg"), sem("s_gln"), sem("s_lf")
        s_btok, s_rtok, s_rbT, s_q, s_tq, s_tqe = (sem("s_btok"), sem("s_rtok"), sem("s_rbT"), sem("s_q"),
                                                  sem("s_tq"), sem("s_tqe"))
        s_proj, s_pev = sem("s_proj"), sem("s_pev")
        s_conv, s_sig, s_qk = sem("s_conv"), sem("s_sig"), sem("s_qk")
        s_vnm, s_vsq, s_vh = sem("s_vnm"), sem("s_vsq"), sem("s_vh")
        s_wspT, s_wspe, s_wspm = sem("s_wspT"), sem("s_wspe"), sem("s_wspm")
        s_sp, s_hg, s_hsq, s_hgr = sem("s_sp"), sem("s_hg"), sem("s_hsq"), sem("s_hgr")
        s_nm, s_s, s_k = sem("s_nm"), sem("s_s"), sem("s_k")
        s_at, s_e, s_wt, s_kw = sem("s_at"), sem("s_e"), sem("s_wt"), sem("s_kw")
        s_p, s_nd = sem("s_p"), sem("s_nd")
        s_xc, s_lsq, s_hm = sem("s_xc"), sem("s_lsq"), sem("s_hm")
        s_hT, s_hTe, s_out, s_h, s_h2, s_hs = (sem("s_hT"), sem("s_hTe"), sem("s_out"), sem("s_h"), sem("s_h2"),
                                              sem("s_hs"))
        s_nT, s_nTe, s_lg, s_lge = sem("s_nT"), sem("s_nTe"), sem("s_lg"), sem("s_lge")
        s_rowst = sems("s_rowst", NT)
        s_trash = sem("s_trash")
        s_rc, s_v8, s_ex = sem("s_rc"), sem("s_v8"), sem("s_ex")
        s_mk, s_cnt, s_nbb, s_bb, s_ug, s_tabs, s_tab = (sem("s_mk"), sem("s_cnt"), sem("s_nbb"), sem("s_bb"),
                                                                sem("s_ug"), sem("s_tabs"), sem("s_tab"))
        s_w = [[sems(f"s_w{par}_{third}_", 4) for third in range(3)] for par in range(2)]
        s_bias = sems("s_bias", 2)
        s_bz, s_bc = sem("s_bz"), sem("s_bc")
        m_xg, m_xp, m_xT = sem("m_xg"), sem("m_xp"), sem("m_xT")
        m_u = sems("m_u", 2)
        m_z, m_gl, m_sg, m_lc, m_t, m_act, m_A, m_aT = (sem(n) for n in ("m_z", "m_gl", "m_sg", "m_lc", "m_t", "m_act",
                                                                        "m_A", "m_aT"))
        m_y, m_yb, m_ys, m_sc, m_is, m_ig = sem("m_y"), sem("m_yb"), sem("m_ys"), sem("m_sc"), sem("m_is"), sem("m_ig")
        f_sq, f_out = sem("f_sq"), sem("f_out")
        f_ready, f_y, f_r = sem("f_ready"), sem("f_y"), sem("f_r")
        s_xr, s_vr, s_hsr, s_lr, s_hr = sem("s_xr"), sem("s_vr"), sem("s_hsr"), sem("s_lr"), sem("s_hr")
        ch = {n: sem(f"chain_{n}") for n in ("dve", "pool", "act")}

        def chained(eng, name):
            n = [0]

            def link(ins):
                n[0] += 1
                ins.then_inc(ch[name], 1)
                eng.wait_ge(ch[name], n[0])
            return link

        def wcols(c0):
            return w_in[0, :, c0:c0 + 512].rearrange("(k p) n -> p k n", p=P)

        def load_up(eng, par, half_k, e, part):
            k = NPART * half_k + part
            src = w_up[0, e].rearrange("e (k p) n -> (e p) k n", p=P)
            eng.dma_start(W[par][:, 2048 * k:2048 * (k + 1)], src[:, k]).then_inc(s_w[par][half_k][part], 16)

        def load_down(eng, par, e, part):
            ks = slice(2 * part, 2 * part + 2)
            src = w_down[0, e].rearrange("e (k p) n -> (e p) k n", p=P)
            eng.dma_start(down(par)[:, ks, :], src[:, ks]).then_inc(s_w[par][2][part], 16)

        NPART = 4
        AHEAD = 2

        def load_all(eng, par, h_or_down, e):
            for part in range(NPART):
                load_down(eng, par, e, part) if h_or_down == 2 else load_up(eng, par, h_or_down, e, part)

        def load_bias(eng, par, e):
            up = b_up[0, e].rearrange("e (a j c) -> (e j) a c", j=H, c=128)
            dn = b_down[0, e].rearrange("e (j c) -> (e j) c", j=H)
            eng.dma_start(bias_up[par][0:P:BT, :].rearrange("p (a c) -> p a c", c=128), up).then_inc(s_bias[par], 16)
            eng.dma_start(bias_dn[par][0:P:BT, :], dn).then_inc(s_bias[par], 16)
        NBIAS = 2 * 16

        block = ctx.enter_context(nc.Block())

        @block.sync
        def _(sp):
            for c in range(NT):
                sp.dma_start(xin[:, c, :], x[0, P * c:P * (c + 1), :]).then_inc(s_tile[c], 16)
            rows = rows_src
            for r0, n, src in ((0, 8, norm1_gain[0].rearrange("(k p) -> k p", p=P)), (8, 4, mlstm_norm_gain[0]),
                               (12, 4, gmlp_out_gain[0].rearrange("(k p) -> k p", p=P)),
                               (16, 8, norm2_gain[0].rearrange("(k p) -> k p", p=P)),
                               (24, 32, conv_qk[0].rearrange("j (f p) -> (j f) p", p=P)), (56, 4, b_spatial[0])):
                sp.dma_start(rows[r0:r0 + n, :], src).then_inc(s_rows, 16)
            for slot, c0 in ((QG, 0), (KG, 512), (VG, 1024), (OG, 1536), (VGG, 2568), (UG, 2056)):
                sp.dma_start(grp[slot], wcols(c0)).then_inc(s_grp[slot], 16)
            sp.wait_ge(s_proj, 8)
            sp.dma_start(wo, w_out[0].rearrange("(k p) n -> p k n", p=P)).then_inc(s_wo, 16)
            sp.wait_ge(s_proj, 24)
            for c in range(NT):
                sp.dma_start(xres[:, c, :], x[0, P * c:P * (c + 1), :]).then_inc(s_xres, 16)
            load_all(sp, 0, 0, slice(0, 1))

            def load_parts(par, third, parts):
                e = slice(par, par + 1)
                for part in parts:
                    load_down(sp, par, e, part) if third == 2 else load_up(sp, par, third, e, part)

            sp.wait_ge(s_p, NT * H)
            sp.wait_ge(s_hm, NT)
            sp.wait_ge(s_hg, NT)
            load_parts(1, 2, (0, 1))
            load_parts(1, 0, (2, 3))
            load_parts(1, 1, (3,))
            for c in range(NT):
                if c == NT - 2:
                    sp.wait_ge(s_hTe, 2 * NT)
                    load_parts(0, 2, (2, 3))
                if c == NT - 1:
                    sp.wait_ge(s_out, 2 * NT)
                    load_parts(0, 1, (0, 1))
                    sp.wait_ge(s_bz, 1)
                    load_bias(sp, 0, slice(0, 1))
                    load_bias(sp, 1, slice(1, 2))
                sp.wait_ge(s_hs, c + 1)
                rows = slice(P * H * c, P * H * (c + 1))
                sp.dma_start(hres[rows, :].rearrange("(p j) n -> p (j n)", j=H), xres[:, c, :]).then_inc(s_rowst[c], 16)
                sp.dma_start(hsrow[rows, :].rearrange("(p j) n -> p (j n)", j=H), HS[:, c % 2, :])\
                    .then_inc(s_rowst[c], 16)
            load_parts(0, 1, (2, 3))
            sp.wait_ge(s_lge, NT)
            load_parts(1, 2, (2, 3))
            for c in range(NT):
                sp.wait_ge(s_rowst[c], 32)
            sp.wait_ge(m_ig, 2)
            rest = [(0, 2, 0), (0, 2, 1), (1, 0, 0), (1, 0, 1), (1, 1, 0), (1, 1, 1), (1, 1, 2)]
            for n, (par, third, part) in enumerate(rest):
                if n >= 2:
                    before = rest[n - 2]
                    sp.wait_ge(s_w[before[0]][before[1]][before[2]], 16)
                if (par, third, part) == (1, 1, 0):
                    sp.wait_ge(s_gtab, 1)
                    sp.wait_ge(s_trash, 32)
                load_parts(par, third, (part,))
            with sp.Fori(1, NE // 2) as i:
                for par in range(2):
                    e = bass.ts(sp.value_load(order_tab[0:1, bass.ts(2 * i + par, 1)], min_val=0, max_val=NE - 1), 1)
                    done = sp.value_load(base_tab[0:1, bass.ts(2 * i + (par - 1), 1)], min_val=1, max_val=NBMAX - 1)
                    for n in range(3 * NPART):
                        third, part = divmod(n, NPART)
                        if part == 0:
                            sp.wait_ge(m_y if third == 2 else m_u[third], done)
                            sp.nop(nofuse=True)
                        if n == 2 * NPART:
                            sp.wait_ge(m_z, done)
                            sp.nop(nofuse=True)
                            sp.wait_ge(m_yb, done)
                            sp.nop(nofuse=True)
                            load_bias(sp, par, e)
                        if n >= AHEAD:
                            t, q = divmod(n - AHEAD, NPART)
                            sp.wait_ge(s_w[par][t][q], 16 * i + 16)
                        load_down(sp, par, e, part) if third == 2 else load_up(sp, par, third, e, part)
            done = sp.value_load(base_tab[0:1, NE - 1:NE], min_val=1, max_val=NBMAX - 1)
            sp.wait_ge(m_y, done)
            sp.nop(nofuse=True)
            sp.dma_start(W[0][:, 4096:5120], final_gain.rearrange("(a n) -> a n", a=1).broadcast_to([P, D]))\
                .then_inc(s_late, 16)
            sp.wait_ge(f_ready, 1)
            for c in range(NT):
                rows = slice(P * H * c, P * H * (c + 1))
                sp.dma_start(W[0][:, D * c:D * (c + 1)], hres[rows, :].rearrange("(p j) n -> p (j n)", j=H))\
                    .then_inc(s_tile[c], 16)
            for c in range(NT):
                sp.wait_ge(f_y, c + 1)
                sp.dma_start(out[0, P * c:P * (c + 1), :], W[0][:, D * c:D * (c + 1)]).then_inc(f_out, 16)
            sp.wait_ge(f_out, 16 * NT)

        @block.gpsimd
        def _(pool):
            link = chained(pool, "pool")
            link(pool.memset(half[:], -0.5))
            link(pool.memset(ident[:], 0.0))
            pool.affine_select(out=ident[:], in_=ident[:], compare_op=ALU.not_equal, fill=1.0, base=0,
                               pattern=[[-1, P]], channel_multiplier=1).then_inc(s_const, 1)
            link(pool.memset(tri, 1.0))
            pool.affine_select(out=tri, in_=tri, compare_op=ALU.is_ge, fill=0.0, base=0,
                               pattern=[[1, P]], channel_multiplier=-1).then_inc(s_const, 1)
            link(pool.memset(maskneg, 0.0))
            pool.affine_select(out=maskneg, in_=maskneg, compare_op=ALU.is_ge, fill=-BIG, base=0,
                               pattern=[[1, P]], channel_multiplier=-1).then_inc(s_const, 1)
            link(pool.memset(sel, 0.0))
            pool.affine_select(out=sel, in_=sel, compare_op=ALU.not_equal, fill=1.0, base=0,
                               pattern=[[-1, H], [0, P]], channel_multiplier=1).then_inc(s_const, 1)

            def rstd(col, n, done):
                link(pool.tensor_scalar(col, col, 1.0 / n, EPS, ALU.mult, ALU.add))
                pool.tensor_tensor(col, col, half[:, 0:col.shape[1]], ALU.pow).then_inc(done, 1)

            for c in range(NT):
                pool.wait_ge(s_xsq, c + 1)
                rstd(st[:, c:c + 1], D, s_xr)
            pool.wait_ge(s_wspe, 1)
            pool.affine_select(out=wspT.rearrange("p (g t) -> p g t", g=H), in_=wspT.rearrange("p (g t) -> p g t", g=H),
                               compare_op=ALU.is_ge, fill=0.0, base=0,
                               pattern=[[0, H], [1, P]], channel_multiplier=-1).then_inc(s_wspm, 1)
            def heads(c):
                pool.wait_ge(s_lsq, H * (c + 1))
                rstd(st[:, 24:28], HD, s_lr)

            def gate_in(c):
                pool.wait_ge(s_vsq, c + 1)
                rstd(st[:, 16 + c:17 + c], DH, s_vr)

            def gate_out(c):
                pool.wait_ge(s_hsq, c + 1)
                rstd(st[:, 20 + c:21 + c], DH, s_hsr)

            for step, c in ((heads, 0), (gate_in, 0), (heads, 1), (heads, 2), (gate_in, 1), (heads, 3), (gate_in, 2),
                            (gate_out, 0), (gate_out, 1), (gate_in, 3), (gate_out, 2), (gate_out, 3)):
                step(c)
            pool.wait_ge(s_p, NT * H)
            pool.wait_ge(s_hm, NT)
            pool.wait_ge(s_hgr, NT)
            pool.memset(misc[:, BIAS0:BIAS0 + 2 * (512 + QC)], 0.0).then_inc(s_bz, 1)
            pool.iota(iota_i, pattern=[[1, NBMAX]], base=0, channel_multiplier=0).then_inc(s_rc, 1)
            pool.iota(tokm_i, pattern=[[H * P, NT]], base=-H * T, channel_multiplier=H).then_inc(s_rc, 1)
            pool.iota(part_i[:, 0:1], pattern=[[0, 1]], base=0, channel_multiplier=1).then_inc(s_rc, 1)
            pool.memset(ones, 1.0).then_inc(s_rc, 1)
            pool.memset(ones16, 1.0).then_inc(s_rc, 1)
            pool.memset(zrow, 0.0).then_inc(s_rc, 1)
            link(pool.memset(stri, 1.0))
            link(pool.affine_select(out=stri, in_=stri, compare_op=ALU.is_gt, fill=0.0, base=0,
                                    pattern=[[1, P]], channel_multiplier=-1))
            pool.tensor_copy(stri16, stri).then_inc(s_rc, 1)
            link(pool.memset(tre, 1.0))
            pool.affine_select(out=tre, in_=tre, compare_op=ALU.is_gt, fill=0.0, base=0,
                               pattern=[[1, 36]], channel_multiplier=-1).then_inc(s_rc, 1)
            for c in range(NT):
                pool.wait_ge(s_h2, c + 1)
                rstd(st[:, 40 + c:41 + c], D, s_hr)
            pool.wait_ge(s_rc, 8)
            for buf in (hres, hsrow):
                pool.dma_start(buf[T * H:NROW, :], zrow).then_inc(s_trash, 16)
            for c in range(NT):
                pool.wait_ge(s_rowst[c], 32)
            pool.wait_ge(s_trash, 32)
            pool.wait_ge(s_tab, 1)
            total = pool.value_load(base_tab[0:1, NE:NE + 1], min_val=NE, max_val=NBMAX - 1)

            def gather(g):
                pool.tensor_copy(idx_g[:], idx_tab[:, bass.ts(g, 1)]).then_inc(m_ig, 1)
                pool.wait_ge(m_ig, g + 1)
                pool.nop(nofuse=True)
                pool.indirect_dma_start(out=xg, out_offset=None, in_=hsrow,
                                        in_offset=bass.IndirectOffsetOnAxis(ap=idx_g[:, 0:1], axis=0))\
                    .then_inc(m_xg, 16)

            def scatter(g):
                pool.tensor_copy(idx_s[:], idx_tab[:, bass.ts(g, 1)]).then_inc(m_is, 1)
                pool.wait_ge(m_is, g + 1)
                pool.wait_ge(m_ys, g + 1)
                pool.nop(nofuse=True)
                pool.indirect_dma_start(out=hres, out_offset=bass.IndirectOffsetOnAxis(ap=idx_s[:, 0:1], axis=0),
                                        in_=ysb, in_offset=None, compute_op=ALU.add).then_inc(m_sc, 16)

            gather(0)
            pool.wait_ge(m_xp, 1)
            gather(1)
            pool.wait_ge(m_xp, 2)
            gather(2)
            scatter(0)
            with pool.Fori(2, total) as g:
                pool.wait_ge(m_xp, g + 1)
                pool.nop(nofuse=True)
                gather(g + 1)
                pool.wait_ge(m_sc, 16 * (g - 1))
                pool.nop(nofuse=True)
                scatter(g - 1)
            final = pool.value_load(base_tab[0:1, NE + 1:NE + 2], min_val=NE - 1, max_val=NBMAX - 2)
            pool.wait_ge(m_sc, 16 * final)
            pool.nop(nofuse=True)
            scatter(final)
            pool.wait_ge(m_sc, 16 * total)
            pool.nop(nofuse=True)
            pool.wait_ge(m_xg, 16 * total + 16)
            pool.nop(nofuse=True)
            pool.memset(idx_s[:], 0).then_inc(f_ready, 1)
            for c in range(NT):
                pool.wait_ge(f_sq, c + 1)
                rstd(st_f[:, c:c + 1], D, f_r)

        @block.scalar
        def _(act):
            link = chained(act, "act")
            act.dma_start(wg, w_in[0, :, 2048:2056].rearrange("(k p) n -> p k n", p=P)).then_inc(s_wg, 16)
            act.dma_start(bg[:, 0:4], b_igate.broadcast_to([P, H])).then_inc(s_gb, 16)
            act.dma_start(bg[:, 4:8], b_fgate.broadcast_to([P, H])).then_inc(s_gb, 16)
            for c in range(NT):
                act.wait_ge(s_tile[c], 16)
                act.activation(qkT[:, 2 * c:2 * c + 2, :], xin[:, c, :].rearrange("p (a n) -> p a n", a=2), ACT.Square,
                               accum_out=st[:, c:c + 1]).then_inc(s_xsq, 1)
            act.dma_start(lng, gmlp_ln_gain.broadcast_to([P, DH])).then_inc(s_small, 16)
            act.dma_start(rb, b_router.broadcast_to([P, NE])).then_inc(s_small, 16)
            act.dma_start(wr, w_router[0].rearrange("(k p) n -> p k n", p=P)).then_inc(s_late, 16)
            act.dma_start(wsp_src, w_spatial[0].rearrange("g t s -> t g s")).then_inc(s_late, 16)
            act.wait_ge(s_gneg, 1)
            link(act.activation(gtmp, gtmp, ACT.Exp))
            act.activation(gtmp, gtmp, ACT.Ln, bias=1.0).then_inc(s_gln, 1)
            for n in range(8):
                act.wait_ge(s_proj, n + 1)
                act.activation(qkpre[:, n, 3:515], B[n % 2][:], ACT.Copy).then_inc(s_pev, 1)
                if n >= 1:
                    f = n - 1
                    act.wait_ge(s_conv, f + 1)
                    if f >= 2:
                        act.wait_ge(s_qk, f - 1)
                    act.activation(sigtmp[:, f % 2, :], qkT[:, f, :], ACT.Sigmoid).then_inc(s_sig, 1)
            act.wait_ge(s_conv, 8)
            act.wait_ge(s_qk, 6)
            act.activation(sigtmp[:, 1, :], qkT[:, 7, :], ACT.Sigmoid).then_inc(s_sig, 1)
            for c in range(NT):
                act.wait_ge(s_proj, 9 + c)
                act.activation(vaug[:, c, :, 0:HD], B[c % 2][:].rearrange("p (h d) -> p h d", h=H), ACT.Copy)\
                    .then_inc(s_pev, 1)
            act.wait_ge(s_tq, 1)
            act.activation(tq, B[5][:, 0:64].rearrange("p (q c h) -> p q c h", q=4, c=NT), ACT.Exp).then_inc(s_tqe, 1)
            act.wait_ge(s_qk, 8)
            act.wait_ge(s_tqe, 1)

            def sigmoid_o(c):
                act.wait_ge(s_proj, 13 + c)
                act.activation(osig[:, c, :], B[c % 2][:], ACT.Sigmoid).then_inc(s_pev, 1)

            def gelu_vg(c):
                act.wait_ge(s_proj, 17 + 2 * c)
                act.activation(vg[:, c, :], B[0][:], ACT.Gelu_apprx_tanh, accum_out=st[:, 8 + c:9 + c])\
                    .then_inc(s_pev, 1)

            def gelu_u(c):
                act.wait_ge(s_proj, 18 + 2 * c)
                act.activation(ug[:, c, :], B[1][:], ACT.Gelu_apprx_tanh).then_inc(s_pev, 1)

            def after_squares():
                if squares[0]:
                    act.wait_ge(*squares[0])

            squares = [None]

            def squares_vg(c):
                act.wait_ge(s_vnm, c + 1)
                after_squares()
                act.activation(vsqj, vg[:, c, :], ACT.Square, bias=st[:, 12 + c:13 + c],
                               accum_out=st[:, 16 + c:17 + c]).then_inc(s_vsq, 1)
                squares[0] = (s_vsq, c + 1)

            def squares_gating(c):
                act.wait_ge(s_hg, c + 1)
                after_squares()
                act.activation(vsqj, hcat[:, c, DH:D], ACT.Square, accum_out=st[:, 20 + c:21 + c]).then_inc(s_hsq, 1)
                squares[0] = (s_hsq, c + 1)

            def exps(c):
                act.wait_ge(s_at, c + 1)
                act.activation(AT[:, c % 2, :], AT[:, c % 2, :], ACT.Exp).then_inc(s_e, 1)
                if c < NT - 1:
                    act.wait_ge(s_k, c + 1)
                    for h in range(H):
                        act.activation(kw[:, c, HD * h:HD * (h + 1)], B[4][:, HD * h:HD * (h + 1)], ACT.Copy,
                                       scale=tq[:, 1, c, h:h + 1]).then_inc(s_kw, 1)

            def squares_heads(c):
                act.wait_ge(s_xc, c + 1)
                after_squares()
                for h in range(H):
                    act.activation(vsqj[:, HD * h:HD * (h + 1)], hcat[:, c, HD * h:HD * (h + 1)], ACT.Square,
                                   accum_out=st[:, 24 + h:25 + h]).then_inc(s_lsq, 1)
                squares[0] = (s_lsq, H * (c + 1))

            def squares_h(c):
                act.wait_ge(s_h, 2 * (c + 1))
                if c >= 1:
                    act.wait_ge(s_h2, c)
                act.activation(sq1k, xres[:, c, :], ACT.Square, accum_out=st[:, 40 + c:41 + c]).then_inc(s_h2, 1)

            for c in range(NT):
                sigmoid_o(c)
                exps(c)
            for step, c in ((gelu_vg, 0), (squares_heads, 0), (squares_vg, 0), (gelu_u, 0), (squares_heads, 1),
                            (gelu_vg, 1), (squares_heads, 2), (squares_vg, 1), (gelu_u, 1), (squares_heads, 3),
                            (gelu_vg, 2), (squares_vg, 2), (squares_gating, 0), (gelu_u, 2), (squares_gating, 1),
                            (gelu_vg, 3), (squares_vg, 3), (squares_gating, 2), (gelu_u, 3), (squares_gating, 3),
                            (squares_h, 0), (squares_h, 1), (squares_h, 2), (squares_h, 3)):
                step(c)
            act.wait_ge(s_v8, 1)
            act.activation(gate, gate, ACT.Exp).then_inc(s_ex, 1)
            act.wait_ge(s_ug, 1)
            act.activation(G32, G16, ACT.Copy).then_inc(s_g32, 1)
            act.wait_ge(s_tab, 1)
            total = act.value_load(base_tab[0:1, NE:NE + 1], min_val=NE, max_val=NBMAX - 1)
            with act.Fori(0, total) as g:
                act.wait_ge(m_gl, g + 1)
                act.activation(sg, z[:, 0:256], ACT.Sigmoid, scale=ALPHA).then_inc(m_sg, 1)
            for c in range(NT):
                act.wait_ge(s_tile[c], 32)
                act.activation(W[0][:, 10240 + D * c:10240 + D * (c + 1)], W[0][:, D * c:D * (c + 1)], ACT.Square,
                               accum_out=st_f[:, c:c + 1]).then_inc(f_sq, 1)

        @block.vector
        def _(dve):
            link = chained(dve, "dve")
            V = nc.vector

            V.memset(qkpre[:, :, 0:3], 0.0)
            link(V.memset(vaug[:, :, :, HD:HD + 1], 1.0))

            def x_norm(c):
                dve.wait_ge(s_xr, c + 1)
                V.tensor_scalar(xin[:, c, :], xin[:, c, :], st[:, c:c + 1], None, ALU.mult).then_inc(s_xs, 1)

            x_norm(0)
            for c in range(NT):
                if c + 1 < NT:
                    x_norm(c + 1)
                if c == 0:
                    dve.wait_ge(s_rT, 1)
                    V.tensor_copy(rowsT, B[5][:, 0:60]).then_inc(s_rTe, 1)
                    dve.wait_ge(s_rTe, 1)
                    V.tensor_copy(n2g[:], rowsT[:, 16:24])
                for hf in range(2):
                    i = 2 * c + hf
                    dve.wait_ge(s_xT, i + 1)
                    V.tensor_tensor(xnT[:, 4 * hf:4 * hf + 4, P * c:P * (c + 1)],
                                    B[6 + hf][:].rearrange("p (k t) -> p k t", k=4),
                                    rowsT[:, 4 * hf:4 * hf + 4].unsqueeze(2).broadcast_to([P, 4, P]), ALU.mult)\
                        .then_inc(s_xTe, 1)
            dve.wait_ge(s_gates, 1)
            dve.wait_ge(s_gb, 32)
            link(V.tensor_tensor(gf, B[4][:, 0:32].rearrange("p (c n) -> p c n", c=NT),
                                 bg.unsqueeze(1).broadcast_to([P, NT, 8]), ALU.add))
            link(V.tensor_scalar(gtmp, gf[:, :, 4:8], -1.0, None, ALU.mult))
            V.tensor_tensor(gtmp, gtmp, gf[:, :, 4:8], ALU.min).then_inc(s_gneg, 1)
            dve.wait_ge(s_gln, 1)
            V.scalar_tensor_tensor(lf.rearrange("p (c h) -> p c h", c=NT), gf[:, :, 4:8], 0.0, gtmp,
                                   ALU.min, ALU.subtract).then_inc(s_lf, 1)

            def conv(f):
                dve.wait_ge(s_pev, f + 1)
                for j in range(4):
                    w = rowsT[:, 24 + 8 * j + f:25 + 8 * j + f]
                    if j == 0:
                        ins = V.tensor_scalar(qkT[:, f, :], qkpre[:, f, 0:T], w, None, ALU.mult)
                    else:
                        ins = V.scalar_tensor_tensor(qkT[:, f, :], qkpre[:, f, j:j + T], w, qkT[:, f, :],
                                                     ALU.mult, ALU.add)
                    if j < 3:
                        link(ins)
                ins.then_inc(s_conv, 1)

            def silu(f):
                dve.wait_ge(s_sig, f + 1)
                V.scalar_tensor_tensor(qkT[:, f, :], qkT[:, f, :], 1.0 if f < 4 else HD ** -0.5,
                                       sigtmp[:, f % 2, :], ALU.mult, ALU.mult).then_inc(s_qk, 1)

            def gates_rows():
                rT = B[5][0:H, :].rearrange("p (c t) -> p c t", c=NT)
                V.memset(cm[0][:, :, 0:64], -BIG)
                V.memset(cm[1][:, :, 0:64], -BIG)
                V.memset(mp[:, 0:1], 0.0)
                dve.wait_ge(s_rbT, 1)
                V.tensor_copy(bT, B[4][0:H, :].rearrange("p (c t) -> p c t", c=NT))
                link(V.tensor_copy(cm[0][:, :, 64:192], rT))
                a, d = 0, 1
                while d < P:
                    link(V.tensor_tensor(cm[1 - a][:, :, 64:192], cm[a][:, :, 64:192], cm[a][:, :, 64 - d:192 - d],
                                         ALU.max))
                    a, d = 1 - a, 2 * d
                for c in range(NT):
                    link(V.tensor_tensor(Ml[:, c:c + 1], mp[:, c:c + 1], cm[a][:, c, 191:192], ALU.max))
                    link(V.tensor_tensor(mp[:, c + 1:c + 2], Ml[:, c:c + 1], bT[:, c, P - 1:P], ALU.add))
                mpb = mp[:, 0:NT].unsqueeze(2).broadcast_to([H, NT, P])
                Mlb = Ml[:, :].unsqueeze(2).broadcast_to([H, NT, P])
                link(V.tensor_tensor(negM, cm[a][:, :, 64:192], mpb, ALU.max))
                link(V.tensor_scalar(negM, negM, -1.0, None, ALU.mult))
                V.tensor_tensor(Q[:, 0], negM, mpb, ALU.add)
                V.tensor_tensor(Q[:, 1], rT, Mlb, ALU.subtract)
                V.tensor_tensor(Q[:, 2], mpb, Mlb, ALU.subtract)
                V.tensor_tensor(Q[:, 3], negM, bT, ALU.subtract).then_inc(s_q, 1)

            for f in range(8):
                if f == 2:
                    dve.wait_ge(s_btok, 1)
                    V.tensor_tensor(rtok.rearrange("p (c h) -> p c h", c=NT), gf[:, :, 0:4],
                                    B[5][:, 0:16].rearrange("p (c h) -> p c h", c=NT), ALU.subtract)\
                        .then_inc(s_rtok, 1)
                if f == 6:
                    gates_rows()
                conv(f)
                if f >= 1:
                    silu(f - 1)
            silu(7)
            dve.wait_ge(s_small, 32)
            dve.wait_ge(s_wspT, 1)
            V.tensor_copy(wspT, B[4][:]).then_inc(s_wspe, 1)
            def vg_mean(c):
                dve.wait_ge(s_pev, 17 + 2 * c)
                V.tensor_scalar(st[:, 12 + c:13 + c], st[:, 8 + c:9 + c], -1.0 / DH, None, ALU.mult).then_inc(s_vnm, 1)

            def vg_norm(c):
                dve.wait_ge(s_vr, c + 1)
                link(V.tensor_scalar(vg[:, c, :], vg[:, c, :], st[:, 12 + c:13 + c], st[:, 16 + c:17 + c],
                                     ALU.add, ALU.mult))
                V.tensor_tensor(vg[:, c, :], vg[:, c, :], lng, ALU.mult).then_inc(s_vh, 1)

            def gating(c):
                dve.wait_ge(s_sp, c + 1)
                dve.wait_ge(s_pev, 18 + 2 * c)
                for g in range(H):
                    ins = V.scalar_tensor_tensor(hcat[:, c, DH + P * g:DH + P * (g + 1)], B[7][:, P * g:P * (g + 1)],
                                                 rowsT[:, 56 + g:57 + g], ug[:, c, P * g:P * (g + 1)], ALU.add, ALU.mult)
                ins.then_inc(s_hg, 1)

            def gating_norm(c):
                dve.wait_ge(s_hsr, c + 1)
                V.tensor_scalar(hcat[:, c, DH:D], hcat[:, c, DH:D], st[:, 20 + c:21 + c], None, ALU.mult)\
                    .then_inc(s_hgr, 1)

            def exponents(c):
                dve.wait_ge(s_nm, c + 1)
                if c >= 2:
                    dve.wait_ge(s_wt, c - 1)
                for h in range(H):
                    ins = V.scalar_tensor_tensor(AT[:, c % 2, P * h:P * (h + 1)], B[2][:, P * h:P * (h + 1)],
                                                 rtok[:, H * c + h:H * c + h + 1], maskneg, ALU.add, ALU.add)
                ins.then_inc(s_at, 1)

            def weights(c):
                dve.wait_ge(s_e, c + 1)
                dve.wait_ge(s_s, c + 1)
                V.tensor_tensor(WT[:, c, :], AT[:, c % 2, :], B[3][:], ALU.mult).then_inc(s_wt, 1)

            def numerators(c):
                if c >= 1:
                    dve.wait_ge(s_hm, c)
                for h in range(H):
                    dve.wait_ge(s_p, H * c + h + 1)
                    b = B[5 + h % 2]
                    if c == 0:
                        V.tensor_copy(Cst[:, h, :], b[:, 258:387])
                        V.tensor_copy(ND[:, h, :], b[:, 0:129]).then_inc(s_nd, 1)
                    else:
                        if c < NT - 1:
                            V.scalar_tensor_tensor(Cst[:, h, :], Cst[:, h, :], tq[:, 2, c, h:h + 1], b[:, 258:387],
                                                   ALU.mult, ALU.add)
                        link(V.tensor_scalar(ND[:, h, :], b[:, 129:258], tq[:, 0, c, h:h + 1], None, ALU.mult))
                        V.tensor_tensor(ND[:, h, :], ND[:, h, :], b[:, 0:129], ALU.add).then_inc(s_nd, 1)
                dve.wait_ge(s_nd, H * (c + 1))

            def heads_norm(c):
                den, neg = st[:, 28:32], st[:, 32:36]
                hc = hcat[:, c, 0:DH].rearrange("p (h d) -> p h d", h=H)
                link(V.scalar_tensor_tensor(den, ND[:, :, HD], -1.0, ND[:, :, HD], ALU.mult, ALU.max))
                link(V.tensor_tensor(den, den, tq[:, 3, c, :], ALU.max))
                link(V.reciprocal(den, den))
                link(V.tensor_tensor(hc, ND[:, :, 0:HD], den.unsqueeze(2).broadcast_to([P, H, HD]), ALU.mult))
                link(V.tensor_reduce(neg, hc, AXX, ALU.add))
                link(V.tensor_scalar(neg, neg, -1.0 / HD, None, ALU.mult))
                V.tensor_tensor(hc, hc, neg.unsqueeze(2).broadcast_to([P, H, HD]), ALU.add).then_inc(s_xc, 1)
                dve.wait_ge(s_xc, c + 1)

            def heads_gate(c):
                dve.wait_ge(s_lr, c + 1)
                for h in range(H):
                    s = slice(HD * h, HD * (h + 1))
                    ins = V.scalar_tensor_tensor(hcat[:, c, s], hcat[:, c, s], st[:, 24 + h:25 + h], osig[:, c, s],
                                                 ALU.mult, ALU.mult)
                ins.then_inc(s_hm, 1)

            def cat_evac(c):
                for hf in range(2):
                    dve.wait_ge(s_hT, 2 * c + hf + 1)
                    V.tensor_tensor(HT[:, c % 2, 4 * hf:4 * hf + 4, :], B[2 + hf][:].rearrange("p (k t) -> p k t", k=4),
                                    rowsT[:, 8 + 4 * hf:12 + 4 * hf].unsqueeze(2).broadcast_to([P, 4, P]), ALU.mult)\
                        .then_inc(s_hTe, 1)

            def residual(c, n):
                dve.wait_ge(s_out, 2 * c + n + 1)
                if c == 0 and n == 0:
                    dve.wait_ge(s_xres, 16 * NT)
                s = slice(512 * n, 512 * (n + 1))
                V.tensor_tensor(xres[:, c, s], B[n][:], xres[:, c, s], ALU.add).then_inc(s_h, 1)

            def second_norm(c):
                dve.wait_ge(s_hr, c + 1)
                if c >= 2:
                    dve.wait_ge(s_rowst[c - 2], 32)
                V.tensor_scalar(HS[:, c % 2, :], xres[:, c, :], st[:, 40 + c:41 + c], None, ALU.mult).then_inc(s_hs, 1)

            def norm_evac(c):
                for hf in range(2):
                    dve.wait_ge(s_nT, 2 * c + hf + 1)
                    V.tensor_tensor(hnT[:, c % 2, 4 * hf:4 * hf + 4, :], B[4 + hf][:].rearrange("p (k t) -> p k t", k=4),
                                    n2g[:, 4 * hf:4 * hf + 4].unsqueeze(2).broadcast_to([P, 4, P]), ALU.mult)\
                        .then_inc(s_nTe, 1)

            def top_experts(c):
                dve.wait_ge(s_lg, c + 1)
                dve.wait_ge(s_hr, c + 1)
                V.scalar_tensor_tensor(logits[:, c, :], B[6][:, 0:NE], st[:, 40 + c:41 + c], rb, ALU.mult, ALU.add)\
                    .then_inc(s_lge, 1)
                dve.wait_ge(s_lge, c + 1)
                link(V.max(v8[:, c, :], logits[:, c, :]))
                link(V.max_index(i8[:, c, :], v8[:, c, :], logits[:, c, :]))
                link(V.tensor_copy(idxf[:, c, :], i8[:, c, 0:TOPK]))
                link(V.tensor_tensor(OH[:, c], iota_f[:, 0:NE].unsqueeze(1).broadcast_to([P, TOPK, NE]),
                                     idxf[:, c, :].unsqueeze(2).broadcast_to([P, TOPK, NE]), ALU.is_equal))
                link(V.tensor_reduce(Mk[:, c, :], OH[:, c].rearrange("p k e -> p e k"), AXX, ALU.add))
                V.tensor_copy(Mk16[:, c, :], Mk[:, c, :]).then_inc(s_mk, 1)

            def heads(c):
                numerators(c)
                heads_norm(c)

            for c in range(NT):
                exponents(c)
                weights(c)
            dve.wait_ge(s_tqe, 1)
            for step, c in ((heads, 0), (vg_mean, 0), (heads_gate, 0), (heads, 1), (heads_gate, 1), (vg_norm, 0),
                            (heads, 2), (vg_mean, 1), (heads_gate, 2), (heads, 3), (vg_norm, 1), (heads_gate, 3),
                            (vg_mean, 2), (gating, 0), (vg_norm, 2), (gating, 1), (gating_norm, 0), (vg_mean, 3),
                            (gating, 2), (vg_norm, 3), (gating_norm, 1), (cat_evac, 0), (gating, 3),
                            (gating_norm, 2), (gating_norm, 3)):
                step(c)
            for c in range(NT):
                residual(c, 0)
                if c + 1 < NT:
                    cat_evac(c + 1)
                if c >= 1:
                    norm_evac(c - 1)
                    top_experts(c - 1)
                residual(c, 1)
                if c == NT - 1:
                    norm_evac(c)
                second_norm(c)
                if c == 0:
                    dve.wait_ge(s_rc, 8)
                    V.tensor_copy(iota_f, iota_i)
                    V.tensor_copy(iota16, iota_i)
                    V.tensor_copy(tokm, tokm_i)
                    V.tensor_copy(spread16, ident[0:BT, 0:BT].unsqueeze(1).broadcast_to([BT, H, BT]))
                    V.tensor_copy(spread, ident[0:BT, 0:BT].unsqueeze(1).broadcast_to([BT, H, BT]))
                    V.tensor_scalar(part_i[:, 1:2], part_i[:, 0:1], 5, None, ALU.logical_shift_right)
                    link(V.tensor_scalar(part_i[:, 2:3], part_i[:, 0:1], 31, None, ALU.bitwise_and))
                    link(V.tensor_copy(partf[:, 1:3], part_i[:, 1:3]))
                    link(V.tensor_scalar(partf[:, 3:4], partf[:, 1:2], float(T * H), None, ALU.add))
                    V.tensor_scalar(partf[:, 2:3], partf[:, 2:3], float(H), None, ALU.mult)
                    link(V.tensor_copy(partf[:, 0:1], part_i[:, 0:1]))
                    V.tensor_scalar(late[:, 1:2], partf[:, 0:1], 1.5, None, ALU.is_gt)
                    link(V.tensor_scalar(expb, ones, partf[:, 0:1], None, ALU.mult))
            top_experts(NT - 1)

            V.tensor_tensor(gate, v8[:, :, 0:TOPK], v8[:, :, 0:1].broadcast_to([P, NT, TOPK]), ALU.subtract)\
                .then_inc(s_v8, 1)
            dve.wait_ge(s_cnt, 1)
            link(V.tensor_scalar(cnt_i[0:NE, 1:2], B[0][0:NE, 0:1], float(BT - 1), None, ALU.add))
            link(V.tensor_scalar(cnt_i[0:NE, 2:3], cnt_i[0:NE, 1:2], 5, None, ALU.logical_shift_right))
            link(V.tensor_scalar(cnt[0:NE, 4:5], cnt_i[0:NE, 2:3], 1.0, None, ALU.max))
            link(V.tensor_scalar(late[0:NE, 0:1], cnt[0:NE, 4:5], 1.0, late[0:NE, 1:2], ALU.is_equal, ALU.mult))
            V.tensor_scalar(nbb[0:NE, P:P + NE], ones[0:NE, 0:NE], late[0:NE, 0:1], None, ALU.mult).then_inc(s_nbb, 1)
            link(V.tensor_scalar(nbb[0:NE, 0:P], ones[0:NE, :], cnt[0:NE, 4:5], None, ALU.mult))
            dve.wait_ge(s_late_e, 1)
            link(V.scalar_tensor_tensor(before[0:NE, 0:NE], B[5][0:NE, 0:NE], late[0:NE, 0:1], tre[0:NE, 0:NE],
                                        ALU.subtract, ALU.add))
            V.tensor_scalar(before[0:NE, 0:NE], before[0:NE, 0:NE], 0.0, 1.0, ALU.max, ALU.min).then_inc(s_before, 1)
            dve.wait_ge(s_bb, 1)
            link(V.tensor_copy(bbs[:, 0:NE], B[1][:, 0:NE]))
            link(V.scalar_tensor_tensor(pos, bbs[:, 0:NE].unsqueeze(1).broadcast_to([P, NT, NE]), float(BT),
                                        B[2][:, 0:128].rearrange("p (c e) -> p c e", c=NT), ALU.mult, ALU.add))
            link(V.tensor_tensor(OHD, OH, pos.unsqueeze(2).broadcast_to([P, NT, TOPK, NE]), ALU.mult))
            link(V.tensor_reduce(dest, OHD, AXX, ALU.add))
            desti = lo.bitcast(i32)
            link(V.tensor_copy(desti, dest))
            hii = hi.bitcast(i32)
            link(V.tensor_scalar(hii, desti, 5, None, ALU.logical_shift_right))
            link(V.tensor_scalar(desti, desti, 31, None, ALU.bitwise_and))
            V.tensor_copy(hi16, hii)
            link(V.tensor_copy(lo16, desti))
            slots = iota16[:, 0:BT].unsqueeze(1).broadcast_to([P, 16, BT])
            blocks = iota16.unsqueeze(1).broadcast_to([P, 16, NBMAX])
            lo_b, hi_b = lo16.unsqueeze(2).broadcast_to([P, 16, BT]), hi16.unsqueeze(2).broadcast_to([P, 16, NBMAX])
            link(V.tensor_tensor(U16, slots, lo_b, ALU.is_equal))
            V.tensor_tensor(UT16.rearrange("p (c k) t -> p c k t", c=NT), U16.rearrange("p (c k) t -> p c k t", c=NT),
                            tokm.unsqueeze(2).unsqueeze(3).broadcast_to([P, NT, TOPK, BT]), ALU.mult)
            V.tensor_tensor(G16, blocks, hi_b, ALU.is_equal).then_inc(s_ug, 1)
            dve.wait_ge(s_place, 1)
            link(V.tensor_copy(late[0:NE, 2:3], B[6][0:NE, 0:1]))
            V.tensor_scalar(behind[0:NE, 0:NE + 1], iota_f[0:NE, 0:NE + 1], late[0:NE, 2:3], None, ALU.is_gt)
            V.tensor_scalar(atp[0:NE, 0:NE], iota_f[0:NE, 0:NE], late[0:NE, 2:3], None, ALU.is_equal).then_inc(s_atp, 1)
            dve.wait_ge(s_tabs, 1)
            V.tensor_copy(tok_s, B[3][0:BT, 0:NBMAX]).then_inc(s_small_tab, 1)
            dve.wait_ge(s_order, 1)
            V.tensor_copy(base_tab[:, 0:NE + 1], B[7][:, 0:NE + 1])
            V.tensor_scalar(base_tab[:, NE + 1:NE + 2], B[7][:, NE:NE + 1], -1.0, None, ALU.add)
            link(V.tensor_copy(order_tab[:], B[7][:, 64:64 + NE]))
            dve.wait_ge(s_spread, 1)
            link(V.tensor_scalar(rowf, B[4][:, 0:NBMAX], 0.0, partf[:, 2:3], ALU.is_equal, ALU.mult))
            V.scalar_tensor_tensor(idx_tab[:], B[4][:, 0:NBMAX], partf[:, 3:4], rowf, ALU.add, ALU.add).then_inc(s_tab, 1)
            dve.wait_ge(s_ex, 1)
            link(V.tensor_reduce(gsum, gate, AXX, ALU.add))
            link(V.reciprocal(grec, gsum))
            link(V.tensor_tensor(gate, gate, grec.unsqueeze(2).broadcast_to([P, NT, TOPK]), ALU.mult))
            V.tensor_tensor(Ug.rearrange("p (c k) t -> p c k t", c=NT), U16.rearrange("p (c k) t -> p c k t", c=NT),
                            gate.unsqueeze(3).broadcast_to([P, NT, TOPK, BT]), ALU.mult).then_inc(s_ug, 1)
            dve.wait_ge(s_tabs, 2)
            V.tensor_copy(gate_s, B[7][0:BT, 0:NBMAX]).then_inc(s_small_tab, 1)
            dve.wait_ge(s_spread, 2)
            V.tensor_copy(gate_tab[:, 1:NBMAX + 1], B[6][:, 0:NBMAX]).then_inc(s_gtab, 1)
            dve.wait_ge(s_gtab, 1)

            def block_front(g, par):
                glu, lin = z[:, 0:256], z[:, 256:512]
                dve.wait_ge(m_u[1], g + 1)
                V.tensor_tensor(z, B[0][:], bias_up[par], ALU.add).then_inc(m_z, 1)
                dve.wait_ge(m_z, g + 1)
                V.tensor_scalar(glu, glu, LIMIT, None, ALU.min).then_inc(m_gl, 1)
                V.tensor_scalar(lin, lin, LIMIT, -LIMIT, ALU.min, ALU.max).then_inc(m_lc, 1)
                dve.wait_ge(m_lc, g + 1)
                V.scalar_tensor_tensor(lin, lin, 1.0, glu, ALU.add, ALU.mult).then_inc(m_t, 1)
                dve.wait_ge(m_t, g + 1)
                dve.wait_ge(m_sg, g + 1)
                V.tensor_tensor(lin, lin, sg, ALU.mult).then_inc(m_act, 1)
                x_evac(g + 1)

            def block_out(g, par):
                dve.wait_ge(m_y, g)
                dve.wait_ge(m_is, g)
                V.tensor_tensor(ysb, B[5][:, 0:QC], bias_dn[par], ALU.add).then_inc(m_yb, 1)
                dve.wait_ge(m_yb, g)
                V.tensor_scalar(ysb, ysb, gate_tab[:, bass.ts(g, 1)], None, ALU.mult).then_inc(m_ys, 1)

            def act_evac(g):
                dve.wait_ge(m_A, g + 1)
                V.tensor_copy(aT, B[3][:, 0:256]).then_inc(m_aT, 1)

            def x_evac(g):
                dve.wait_ge(m_xp, g + 1)
                V.tensor_tensor(xT.rearrange("p (h j t) -> p h j t", h=2, j=H), B[2][:, 0:256].rearrange("p (h j t) -> p h j t", h=2, j=H),
                                n2g[:].rearrange("p (j h) -> p h j", h=2).unsqueeze(3).broadcast_to([P, 2, H, BT]), ALU.mult)\
                    .then_inc(m_xT, 1)

            dve.wait_ge(s_tab, 1)
            x_evac(0)

            def expert(par, i, first, last):
                dve.wait_ge(s_bias[par], NBIAS * i + NBIAS)
                dve.nop(nofuse=True)
                V.stream_shuffle(bias_all[par], bias_all[par], [0] * BT).then_inc(s_bc, 1)
                dve.wait_ge(s_bc, 2 * i + (par + 1))
                dve.nop(nofuse=True)
                lead = not isinstance(first, int)
                block_front(first, par)
                if lead:
                    block_out(first, 1 - par)
                act_evac(first)
                with dve.If_lt(dve.to_reg(first + 1), dve.to_reg(last)):
                    with dve.Fori(first + 1, last) as g:
                        block_front(g, par)
                        block_out(g, par)
                        act_evac(g)

            def base(e):
                return dve.value_load(base_tab[0:1, bass.ts(e, 1)], min_val=1, max_val=NBMAX - 1)

            expert(0, 0, 0, base(1))
            expert(1, 0, base(1), base(2))
            with dve.Fori(1, NE // 2) as i:
                for par in range(2):
                    expert(par, i, base(2 * i + par), base(2 * i + par + 1))
            block_out(dve.value_load(base_tab[0:1, NE:NE + 1], min_val=NE, max_val=NBMAX - 1), 1)
            dve.wait_ge(s_late, 48)
            for c in range(NT):
                dve.wait_ge(f_r, c + 1)
                tile = W[0][:, D * c:D * (c + 1)]
                V.scalar_tensor_tensor(tile, tile, st_f[:, c:c + 1], W[0][:, 4096:5120], ALU.mult, ALU.mult)\
                    .then_inc(f_y, 1)

        @block.tensor
        def _(pe):
            mm = nc.tensor.matmul

            def project(n, lhs, rhs, slot):
                pe.wait_ge(s_grp[slot], 16)
                if n >= 2:
                    pe.wait_ge(s_pev, n - 1)
                for k in range(NK):
                    ins = mm(B[n % 2][:], lhs(k), rhs(k), start=(k == 0), stop=(k == NK - 1))
                ins.then_inc(s_proj, 1)

            def tokens(n, c, slot):
                project(n, lambda k: xnT[:, k, P * c:P * (c + 1)], lambda k: grp[slot][:, k, :], slot)

            pe.wait_ge(s_const, 1)
            pe.wait_ge(s_rows, 96)
            nc.tensor.transpose(B[5][:, 0:60], rows_src, ident[0:60, 0:60]).then_inc(s_rT, 1)
            for c in range(NT):
                pe.wait_ge(s_xs, c + 1)
                for hf in range(2):
                    if c >= 1:
                        pe.wait_ge(s_xTe, 2 * c + hf - 1)
                    for k in range(4):
                        ins = nc.tensor.transpose(B[6 + hf][:, P * k:P * (k + 1)],
                                                  xin[:, c, P * (4 * hf + k):P * (4 * hf + k + 1)], ident[:])
                    ins.then_inc(s_xT, 1)
            pe.wait_ge(s_wg, 16)
            pe.wait_ge(s_xTe, 2 * NT)
            for c in range(NT):
                for k in range(NK):
                    ins = mm(B[4][:, 8 * c:8 * (c + 1)], xnT[:, k, P * c:P * (c + 1)], wg[:, k, :],
                             start=(k == 0), stop=(k == NK - 1))
            ins.then_inc(s_gates, 1)
            for f in range(8):
                slot, col = (QG, KG)[f // 4], 128 * (f % 4)
                project(f, lambda k: grp[slot][:, k, col:col + 128], lambda k: xnT[:, k, :], slot)
                if f == 1:
                    pe.wait_ge(s_lf, 1)
                    pe.wait_ge(s_const, 4)
                    mm(B[5][:, 0:16], tri, lf, start=True, stop=True).then_inc(s_btok, 1)
                if f == 3:
                    pe.wait_ge(s_rtok, 1)
                    for c in range(NT):
                        mm(B[5][0:H, P * c:P * (c + 1)], rtok[:, H * c:H * (c + 1)], ident[:], start=True, stop=True)
                        ins = mm(B[4][0:H, P * c:P * (c + 1)], lf[:, H * c:H * (c + 1)], tri, start=True, stop=True)
                    ins.then_inc(s_rbT, 1)
            for c in range(NT):
                tokens(8 + c, c, VG)
            pe.wait_ge(s_q, 1)
            for q in range(4):
                for c in range(NT):
                    o = 16 * q + 4 * c
                    ins = mm(B[5][:, o:o + 4], Q[:, q, c, :], ident[0:H, 0:H], start=True, stop=True)
            ins.then_inc(s_tq, 1)
            pe.wait_ge(s_late, 32)
            for g in range(H):
                ins = nc.tensor.transpose(B[4][:, P * g:P * (g + 1)], wsp_src[:, g, :], ident[:])
            ins.then_inc(s_wspT, 1)
            def spatial(c):
                pe.wait_ge(s_vh, c + 1)
                pe.wait_ge(*((s_hg, c) if c >= 1 else (s_wspm, 1)))
                for g in range(H):
                    ins = mm(B[7][:, P * g:P * (g + 1)], wspT[:, P * g:P * (g + 1)], vg[:, c, P * g:P * (g + 1)],
                             start=True, stop=True)
                ins.then_inc(s_sp, 1)

            def chunk_products(c):
                t = slice(P * c, P * (c + 1))
                if c >= 1:
                    pe.wait_ge(s_at, c)
                for h in range(H):
                    ins = mm(B[2][:, P * h:P * (h + 1)], sel[:, h, :], negM[:, c, :], start=True, stop=True)
                ins.then_inc(s_nm, 1)
                if c >= 1:
                    pe.wait_ge(s_wt, c)
                for h in range(H):
                    ins = mm(B[3][:, P * h:P * (h + 1)], qkT[:, H + h, t], qkT[:, h, t], start=True, stop=True)
                ins.then_inc(s_s, 1)
                if c < NT - 1:
                    pe.wait_ge(*((s_kw, H * c) if c >= 1 else (s_wspe, 1)))
                    for h in range(H):
                        ins = nc.tensor.transpose(B[4][:, P * h:P * (h + 1)], qkT[:, H + h, t], ident[:])
                    ins.then_inc(s_k, 1)

            def chunk_heads(c):
                pe.wait_ge(s_wt, c + 1)
                if c < NT - 1:
                    pe.wait_ge(s_kw, H * (c + 1))
                for h in range(H):
                    i = H * c + h
                    if i >= 2:
                        pe.wait_ge(s_nd, i - 1)
                    b = B[5 + h % 2]
                    ins = mm(b[:, 0:129], WT[:, c, P * h:P * (h + 1)], vaug[:, c, h, :], start=True, stop=True)
                    if c >= 1:
                        ins = mm(b[:, 129:258], qkT[:, h, P * c:P * (c + 1)], Cst[:, h, :], start=True, stop=True)
                    if c < NT - 1:
                        ins = mm(b[:, 258:387], kw[:, c, HD * h:HD * (h + 1)], vaug[:, c, h, :], start=True, stop=True)
                    ins.then_inc(s_p, 1)

            def cat(c):
                pe.wait_ge(s_hm, c + 1)
                pe.wait_ge(s_hgr, c + 1)
                if c >= 1:
                    pe.wait_ge(s_hTe, 2 * c)
                for hf in range(2):
                    for k in range(4):
                        ins = nc.tensor.transpose(B[2 + hf][:, P * k:P * (k + 1)],
                                                  hcat[:, c, P * (4 * hf + k):P * (4 * hf + k + 1)], ident[:])
                    ins.then_inc(s_hT, 1)

            def project_out(c):
                pe.wait_ge(s_hTe, 2 * c + 2)
                for n in range(2):
                    if c >= 1:
                        pe.wait_ge(s_h, 2 * (c - 1) + n + 1)
                    for k in range(NK):
                        ins = mm(B[n][:], HT[:, c % 2, k, :], wo[:, k, 512 * n:512 * (n + 1)],
                                 start=(k == 0), stop=(k == NK - 1))
                    ins.then_inc(s_out, 1)
                    if n == 0 and c + 1 < NT:
                        cat(c + 1)
                    if n == 0 and c >= 1:
                        router(c - 1)

            def router(c):
                if c >= 1:
                    pe.wait_ge(s_nTe, 2 * c)
                for hf in range(2):
                    pe.wait_ge(s_h, 2 * c + hf + 1)
                    for k in range(4):
                        ins = nc.tensor.transpose(B[4 + hf][:, P * k:P * (k + 1)],
                                                  xres[:, c, P * (4 * hf + k):P * (4 * hf + k + 1)], ident[:])
                    ins.then_inc(s_nT, 1)
                if c >= 1:
                    pe.wait_ge(s_lge, c)
                for k in range(NK):
                    if k % 4 == 0:
                        pe.wait_ge(s_nTe, 2 * c + k // 4 + 1)
                    ins = mm(B[6][:, 0:NE], hnT[:, c % 2, k, :], wr[:, k, :], start=(k == 0), stop=(k == NK - 1))
                ins.then_inc(s_lg, 1)

            pe.wait_ge(s_qk, 8)
            for c in range(NT):
                tokens(12 + c, c, OG)
                chunk_products(c)
            for c in range(NT):
                tokens(16 + 2 * c, c, VGG)
                if c < 2:
                    chunk_heads(2 * c)
                else:
                    spatial(2 * (c - 2))
                tokens(17 + 2 * c, c, UG)
                if c < 2:
                    chunk_heads(2 * c + 1)
                elif c == 2:
                    spatial(1)
            cat(0)
            spatial(3)
            pe.wait_ge(s_pev, 24)
            pe.wait_ge(s_wo, 16)
            for c in range(NT):
                project_out(c)
            router(NT - 1)
            pe.wait_ge(s_rc, 8)
            pe.wait_ge(s_mk, NT)
            for c in range(NT):
                mm(B[0][0:NE, 0:1], Mk16[:, c, :], ones16[:, 0:1], start=(c == 0), stop=(c == NT - 1))
            for c in range(NT):
                for d in range(c + 1):
                    ins = mm(B[2][:, NE * c:NE * (c + 1)], stri16 if d == c else ones16, Mk16[:, d, :],
                             start=(d == 0), stop=(d == c))
            ins.then_inc(s_cnt, 1)
            pe.wait_ge(s_nbb, 1)
            mm(B[5][0:NE, 0:NE], nbb[0:NE, P:P + NE], ident[0:NE, 0:NE], start=True, stop=True).then_inc(s_late_e, 1)
            pe.wait_ge(s_before, 1)
            mm(B[1][:, 0:NE], nbb[0:NE, 0:P], before[0:NE, 0:NE], start=True, stop=True).then_inc(s_bb, 1)
            mm(B[6][0:NE, 0:1], before[0:NE, 0:NE], ones[0:NE, 0:1], start=True, stop=True).then_inc(s_place, 1)
            def table(U, G, bank):
                for a in range(NT * TOPK):
                    ins = mm(B[bank][0:BT, 0:NBMAX], U[:, a, :], G[:, a, :], start=(a == 0), stop=(a == NT * TOPK - 1))
                ins.then_inc(s_tabs, 1)

            def spread_table(n, sp, small, bank):
                pe.wait_ge(s_small_tab, n)
                mm(B[bank][:, 0:NBMAX], sp.rearrange("p j t -> p (j t)"), small, start=True, stop=True)\
                    .then_inc(s_spread, 1)

            pe.wait_ge(s_ug, 1)
            table(UT16, G16, 3)
            pe.wait_ge(s_atp, 1)
            mm(B[7][:, 0:NE + 1], nbb[0:NE, 0:P], behind[0:NE, 0:NE + 1], start=True, stop=True)
            mm(B[7][:, 64:64 + NE], expb[0:NE, :], atp[0:NE, 0:NE], start=True, stop=True).then_inc(s_order, 1)
            spread_table(1, spread16, tok_s, 4)
            pe.wait_ge(s_ug, 2)
            pe.wait_ge(s_g32, 1)
            table(Ug, G32, 7)
            spread_table(2, spread, gate_s, 6)

            def transpose_block(g):
                pe.wait_ge(m_xg, 16 * g + 16)
                for h in range(2):
                    ins = nc.tensor.transpose(B[2][:, P * h:P * (h + 1)], xg[:, P * h:P * (h + 1)], ident[:])
                ins.then_inc(m_xp, 1)

            def transpose_act(g):
                pe.wait_ge(m_act, g)
                for h in range(2):
                    ins = nc.tensor.transpose(B[3][:, P * h:P * (h + 1)], z[:, 256 + P * h:256 + P * (h + 1)], ident[:])
                ins.then_inc(m_A, 1)

            def block_up(g, par, before, loaded):
                pe.wait_ge(m_xT, g + 1)
                if before:
                    pe.wait_ge(m_z, g)
                for k in range(NK):
                    if loaded is not None:
                        pe.wait_ge(s_w[par][k // 4][k % 4], loaded)
                        pe.nop(nofuse=True)
                    if k == 2 and before:
                        transpose_act(g)
                    o = P * (k % 2) + BT * (k // 2)
                    for j in range(H):
                        ins = mm(B[0][BT * j:BT * (j + 1), :].rearrange("p (g h c) -> p g h c", g=2, h=2),
                                 xT[:, o:o + BT], up(par)[:, k, :, :, P * j:P * (j + 1)],
                                 start=(k == 0), stop=(k == NK - 1))
                    if k % 4 == 3:
                        ins.then_inc(m_u[k // 4], 1)

            def block_down(g, par, loaded, more):
                pe.wait_ge(m_aT, g)
                for part in range(NPART):
                    pe.wait_ge(s_w[par][2][part], loaded)
                for h in range(2):
                    if h == 1 and more:
                        transpose_block(g + 1)
                    for q in range(H):
                        for j in range(H):
                            ins = mm(B[5][BT * j:BT * (j + 1), 0:QC], aT[:, P * h + BT * q:P * h + BT * (q + 1)],
                                     down(par)[:, H * h + q, QC * j:QC * (j + 1)],
                                     start=(h == 0 and q == 0), stop=(h == 1 and q == H - 1))
                ins.then_inc(m_y, 1)

            def expert(par, i, first, last):
                lead = not isinstance(first, int)
                block_up(first, par, lead, 16 * i + 16)
                if lead:
                    block_down(first, 1 - par, 16 * i + 16 * par, True)
                else:
                    transpose_block(1)
                with pe.If_lt(pe.to_reg(first + 1), pe.to_reg(last)):
                    with pe.Fori(first + 1, last) as g:
                        block_up(g, par, True, None)
                        block_down(g, par, 16 * i + 16, True)

            def base(e):
                return pe.value_load(base_tab[0:1, bass.ts(e, 1)], min_val=1, max_val=NBMAX - 1)

            pe.wait_ge(s_tab, 1)
            transpose_block(0)
            expert(0, 0, 0, base(1))
            expert(1, 0, base(1), base(2))
            with pe.Fori(1, NE // 2) as i:
                for par in range(2):
                    expert(par, i, base(2 * i + par), base(2 * i + par + 1))
            total = pe.value_load(base_tab[0:1, NE:NE + 1], min_val=NE, max_val=NBMAX - 1)
            transpose_act(total)
            block_down(total, 1, 16 * (NE // 2), False)


_INS = ["x", "norm1_gain", "w_in", "conv_qk", "b_igate", "b_fgate", "mlstm_norm_gain", "gmlp_ln_gain",
        "w_spatial", "b_spatial", "gmlp_out_gain", "w_out", "norm2_gain", "w_router", "b_router",
        "w_up", "b_up", "w_down", "b_down", "final_gain"]
_OUTS = [((1, T, D), "float32")]


def kernel(**inputs):
    import numpy as _np
    import concourse.bacc as _bacc
    from concourse import mybir as _mybir
    from concourse.bass_utils import run_bass_kernel_spmd as _run

    nc = _bacc.Bacc("TRN2", target_bir_lowering=False, num_devices=1)
    arrays, args = {}, []
    for name in _INS:
        a = _np.ascontiguousarray(inputs[name])
        arrays[f"in_{name}_dram"] = a
        args.append(nc.dram_tensor(f"in_{name}_dram", a.shape, _mybir.dt.from_np(a.dtype), kind="ExternalInput").ap())
    for i, (shape, dtype) in enumerate(_OUTS):
        dt = _mybir.dt.from_np(_np.dtype(dtype))
        args.append(nc.dram_tensor(f"out_{i}_dram", shape, dt, kind="ExternalOutput").ap())
    hybrid_layer(nc, *args)
    r = _run(nc, [arrays], core_ids=[0])
    return r.results[0]["out_0_dram"]
```
